# Optimizing a Trainium2 kernel written in Bass

```python
import math
import jax, jax.numpy as jnp
from jax import lax
import numpy as np

D_MODEL = 1024
BATCH = 1
SEQ = 256
DEPTH = 2

N_MIXERS = 3
D_FF = 2816
N_SUB = 3
EPS = 1e-6
A_HEADS = 8
A_DK = D_MODEL // A_HEADS
A_DV = D_MODEL // A_HEADS
A_CHUNK = 64
B_HEADS = 8
B_DH = D_MODEL // (2 * B_HEADS)
B_ROT = B_DH // 4
ROPE_THETA = 500000.0
Q_BLOCK = 128
C_WIDTH = 3
N_A = (DEPTH + 2) // N_MIXERS
N_B = (DEPTH + 1) // N_MIXERS
N_C = DEPTH // N_MIXERS


def rmsnorm(x, g):
    xf = x.astype(jnp.float32)
    y = xf * lax.rsqrt(jnp.mean(xf * xf, axis=-1, keepdims=True) + EPS)
    return (y * g.astype(jnp.float32)).astype(x.dtype)

def swiglu(h, wi, wo):
    gt, up = jnp.split(h @ wi, 2, axis=-1)
    return (jax.nn.silu(gt) * up) @ wo

def partial_rope(x, cos, sin):
    xr, xp = x[..., :B_ROT], x[..., B_ROT:]
    x1 = xr[..., :B_ROT // 2].astype(jnp.float32)
    x2 = xr[..., B_ROT // 2:].astype(jnp.float32)
    rot = jnp.concatenate([x1 * cos - x2 * sin, x2 * cos + x1 * sin], axis=-1)
    return jnp.concatenate([rot.astype(x.dtype), xp], axis=-1)

def hgrn2_mixer(h, w_in, w_out, lb, onorm_g):
    Bn, S, _ = h.shape
    nc = S // A_CHUNK
    q, fz, i, g = jnp.split(h @ w_in, 4, axis=-1)
    q = jax.nn.silu(q).astype(jnp.float32)
    f = lb.astype(jnp.float32) + (1.0 - lb.astype(jnp.float32)) * jax.nn.sigmoid(fz.astype(jnp.float32))
    logf = jnp.log(f)
    k = 1.0 - f

    def heads(t, dh):
        t = t.astype(jnp.float32).reshape(Bn, nc, A_CHUNK, A_HEADS, dh)
        return t.transpose(1, 0, 3, 2, 4)

    causal = jnp.tril(jnp.ones((A_CHUNK, A_CHUNK), dtype=bool))

    def step(state, inp):
        q_c, k_c, v_c, lf_c = inp
        b = jnp.cumsum(lf_c, axis=2)
        inter = jnp.einsum('bhtk,bhkv->bhtv', q_c * jnp.exp(b), state)
        diff = b[:, :, :, None, :] - b[:, :, None, :, :]
        decay = jnp.exp(jnp.where(causal[:, :, None], diff, -jnp.inf))
        att = jnp.einsum('bhtk,bhsk,bhtsk->bhts', q_c, k_c, decay)
        intra = jnp.einsum('bhts,bhsv->bhtv', att, v_c)
        b_last = b[:, :, -1]
        new_state = jnp.exp(b_last)[..., None] * state + jnp.einsum(
            'bhsk,bhsv->bhkv', k_c * jnp.exp(b_last[:, :, None] - b), v_c)
        return new_state, inter + intra

    s0 = jnp.zeros((Bn, A_HEADS, A_DK, A_DV), jnp.float32)
    _, o = lax.scan(step, s0, (heads(q, A_DK), heads(k, A_DK), heads(i, A_DV), heads(logf, A_DK)))
    o = o.transpose(1, 0, 3, 2, 4).reshape(Bn, S, A_HEADS, A_DV)
    o = rmsnorm(o, onorm_g) * jax.nn.silu(g.astype(jnp.float32).reshape(Bn, S, A_HEADS, A_DV))
    return o.reshape(Bn, S, D_MODEL).astype(h.dtype) @ w_out

def diff_attention_mixer(h, w_in, w_out, qk_g, lam_p, subln_g, cos, sin, lambda_init):
    Bn, S, _ = h.shape
    q, k, v = jnp.split(h @ w_in, 3, axis=-1)
    q = q.reshape(Bn, S, B_HEADS, 2, B_DH)
    k = k.reshape(Bn, S, B_HEADS, 2, B_DH)
    v = v.reshape(Bn, S, B_HEADS, 2 * B_DH).transpose(0, 2, 1, 3)
    q = partial_rope(rmsnorm(q, qk_g[0]), cos, sin).transpose(0, 2, 3, 1, 4)
    k = partial_rope(rmsnorm(k, qk_g[1]), cos, sin).transpose(0, 2, 3, 1, 4)
    lp = lam_p.astype(jnp.float32)
    lam = jnp.exp(jnp.sum(lp[0] * lp[1])) - jnp.exp(jnp.sum(lp[2] * lp[3])) + lambda_init
    scale = B_DH ** -0.5
    outs = []
    for blk in range(S // Q_BLOCK):
        s0 = blk * Q_BLOCK
        s1 = s0 + Q_BLOCK
        sc = jnp.einsum('bhcqd,bhckd->bhcqk', q[:, :, :, s0:s1], k[:, :, :, :s1]).astype(jnp.float32) * scale
        mask = (s0 + jnp.arange(Q_BLOCK))[:, None] >= jnp.arange(s1)[None, :]
        p = jax.nn.softmax(jnp.where(mask, sc, -jnp.inf), axis=-1)
        a = p[:, :, 0] - lam * p[:, :, 1]
        outs.append(jnp.einsum('bhqk,bhkv->bhqv', a.astype(v.dtype), v[:, :, :s1]))
    o = jnp.concatenate(outs, axis=2)
    o = rmsnorm(o, subln_g) * (1.0 - lambda_init)
    return o.transpose(0, 2, 1, 3).reshape(Bn, S, D_MODEL) @ w_out

def short_conv_mixer(h, w_in, conv_w, w_out):
    bg, cg, u = jnp.split(h @ w_in, 3, axis=-1)
    u = cg * u
    up = jnp.pad(u, ((0, 0), (C_WIDTH - 1, 0), (0, 0)))
    y = conv_w[0] * up[:, :-2] + conv_w[1] * up[:, 1:-1] + conv_w[2] * up[:, 2:]
    return (bg * y) @ w_out

def first_inputs(seed: int = 0) -> dict:
    key = jax.random.key(seed)
    ks = jax.random.split(key, 24)
    D, F = D_MODEL, D_FF
    sD, sF = D ** -0.5, F ** -0.5
    n = jax.random.normal
    return {
        "x": n(ks[0], (BATCH, SEQ, D), jnp.float32),
        "c": n(ks[1], (BATCH, D), jnp.float32),
        "positions": (jnp.arange(SEQ, dtype=jnp.int32)[None, :]
                      + jax.random.randint(ks[2], (BATCH, 1), 0, 4096, dtype=jnp.int32)),
        "ada_w": n(ks[3], (DEPTH, D, 3 * N_SUB * D), jnp.float32) * (0.2 * sD),
        "ada_b": n(ks[4], (DEPTH, 3 * N_SUB * D), jnp.float32) * 0.02,
        "norm_g": 1.0 + 0.02 * n(ks[5], (DEPTH, N_SUB, D), jnp.float32),
        "ffn_wi": n(ks[6], (DEPTH, 2, D, 2 * F), jnp.float32) * sD,
        "ffn_wo": n(ks[7], (DEPTH, 2, F, D), jnp.float32) * sF,
        "a_w_in": n(ks[8], (N_A, D, 4 * D), jnp.float32) * sD,
        "a_w_out": n(ks[9], (N_A, D, D), jnp.float32) * sD,
        "a_lb": 0.5 * n(ks[10], (N_A, D), jnp.float32),
        "a_onorm": 1.0 + 0.02 * n(ks[11], (N_A, A_DV), jnp.float32),
        "b_w_in": n(ks[12], (N_B, D, 3 * D), jnp.float32) * sD,
        "b_w_out": n(ks[13], (N_B, D, D), jnp.float32) * sD,
        "b_qk_g": 1.0 + 0.02 * n(ks[14], (N_B, 2, B_DH), jnp.float32),
        "b_lam": 0.1 * n(ks[15], (N_B, 4, B_DH), jnp.float32),
        "b_subln": 1.0 + 0.02 * n(ks[16], (N_B, 2 * B_DH), jnp.float32),
        "c_w_in": n(ks[17], (N_C, D, 3 * D), jnp.float32) * sD,
        "c_conv": n(ks[18], (N_C, C_WIDTH, D), jnp.float32) * (C_WIDTH ** -0.5),
        "c_w_out": n(ks[19], (N_C, D, D), jnp.float32) * sD,
    }

def first_block(x, c, positions, ada_w, ada_b, norm_g, ffn_wi, ffn_wo,
              a_w_in, a_w_out, a_lb, a_onorm,
              b_w_in, b_w_out, b_qk_g, b_lam, b_subln,
              c_w_in, c_conv, c_w_out):
    Bn, S, D = x.shape
    inv_freq = ROPE_THETA ** (-jnp.arange(0, B_ROT, 2, dtype=jnp.float32) / B_ROT)
    ang = positions.astype(jnp.float32)[..., None] * inv_freq
    cos = jnp.cos(ang)[:, :, None, None, :]
    sin = jnp.sin(ang)[:, :, None, None, :]
    lb_sm = jax.nn.softmax(a_lb.astype(jnp.float32), axis=0)
    lb_all = jnp.cumsum(lb_sm, axis=0) - lb_sm[0]
    c_act = jax.nn.silu(c)

    for l in range(DEPTH):
        mod = (c_act @ ada_w[l] + ada_b[l]).reshape(Bn, N_SUB, 3, 1, D)

        def pre(h, j):
            return rmsnorm(h, norm_g[l, j]) * (1.0 + mod[:, j, 1]) + mod[:, j, 0]

        x = x + 0.5 * (1.0 + mod[:, 0, 2]) * swiglu(pre(x, 0), ffn_wi[l, 0], ffn_wo[l, 0])
        h = pre(x, 1)
        kind, idx = l % N_MIXERS, l // N_MIXERS
        if kind == 0:
            y = hgrn2_mixer(h, a_w_in[idx], a_w_out[idx], lb_all[idx], a_onorm[idx])
        elif kind == 1:
            lambda_init = 0.8 - 0.6 * math.exp(-0.3 * l)
            y = diff_attention_mixer(h, b_w_in[idx], b_w_out[idx], b_qk_g[idx], b_lam[idx],
                                     b_subln[idx], cos, sin, lambda_init)
        else:
            y = short_conv_mixer(h, c_w_in[idx], c_conv[idx], c_w_out[idx])
        x = x + (1.0 + mod[:, 1, 2]) * y
        x = x + 0.5 * (1.0 + mod[:, 2, 2]) * swiglu(pre(x, 2), ffn_wi[l, 1], ffn_wo[l, 1])
    return x


HEAD_DIM = 64
NSA_HEADS = 8
NSA_KV_GROUPS = 2
NSA_HPG = NSA_HEADS // NSA_KV_GROUPS
NSA_WIDTH = NSA_HEADS * HEAD_DIM
KV_WIDTH = NSA_KV_GROUPS * HEAD_DIM
CMP_BLOCK = 32
CMP_STRIDE = 16
CMP_HIDDEN = 128
SEL_BLOCK = 64
SEL_TOPK = 16
WINDOW = 512
GM_GROUPS = 8
GM_CHUNK = 128
GM_WIDTH = GM_GROUPS * HEAD_DIM
N_BRANCH = 2
ROPE_THETA_2 = 10000.0
NEG = -1e30
FORCE = 1e4
IN_SIZES = [NSA_WIDTH, 6 * KV_WIDTH, 3 * NSA_HEADS, 2 * GM_WIDTH, D_MODEL, D_MODEL]
IN_WIDTH = sum(IN_SIZES)
IN_SPLITS = np.cumsum(IN_SIZES)[:-1].tolist()


def _rmsnorm(x, g):
    x32 = x.astype(jnp.float32)
    y = x32 * lax.rsqrt(jnp.mean(x32 * x32, axis=-1, keepdims=True) + EPS)
    return y.astype(x.dtype) * g

def _layernorm(x, g, b):
    x32 = x.astype(jnp.float32)
    mu = jnp.mean(x32, axis=-1, keepdims=True)
    var = jnp.mean(jnp.square(x32 - mu), axis=-1, keepdims=True)
    return ((x32 - mu) * lax.rsqrt(var + EPS)).astype(x.dtype) * g + b

def _rope_tables(pos):
    inv = 1.0 / (ROPE_THETA_2 ** (jnp.arange(0, HEAD_DIM, 2, dtype=jnp.float32) / HEAD_DIM))
    ang = pos.astype(jnp.float32)[:, None] * inv[None, :]
    return jnp.cos(ang), jnp.sin(ang)

def _rope(x, cos, sin):
    x32 = x.astype(jnp.float32)
    x1, x2 = jnp.split(x32, 2, axis=-1)
    c = cos[None, :, None, :]
    s = sin[None, :, None, :]
    return jnp.concatenate([x1 * c - x2 * s, x2 * c + x1 * s], axis=-1).astype(x.dtype)

def _modulate(xn, shift, scale):
    return xn * (1.0 + scale) + shift

def _swiglu(x, w_in, w_out):
    a, b = jnp.split(x @ w_in, 2, axis=-1)
    return (jax.nn.silu(a) * b) @ w_out

def _nsa(q, k_cmp, v_cmp, k_sel, v_sel, k_win, v_win, gates, pe, w1, w2):
    B, S = q.shape[0], q.shape[1]
    G, HG = NSA_KV_GROUPS, NSA_HPG
    scale = HEAD_DIM ** -0.5
    pos = jnp.arange(S, dtype=jnp.int32)
    cos, sin = _rope_tables(pos)
    qr = _rope(q, cos, sin).reshape(B, S, G, HG, HEAD_DIM)

    n_cmp = (S - CMP_BLOCK) // CMP_STRIDE + 1
    starts = jnp.arange(n_cmp, dtype=jnp.int32) * CMP_STRIDE
    win_idx = starts[:, None] + jnp.arange(CMP_BLOCK, dtype=jnp.int32)[None, :]

    def compress(t, j):
        blk = t[:, win_idx] + pe[j][None, None, :, None, :]
        h = jax.nn.silu(jnp.einsum('bnlgd,ldf->bngf', blk, w1[j]))
        return h @ w2[j]

    kc = compress(k_cmp, 0)
    vc = compress(v_cmp, 1)
    cend = starts + CMP_BLOCK - 1
    ccos, csin = _rope_tables(cend)
    kc = _rope(kc, ccos, csin)
    s_c = jnp.einsum('bsghd,bngd->bsghn', qr, kc).astype(jnp.float32) * scale
    m_c = (cend[None, :] <= pos[:, None])[None, :, None, None, :]
    p_c = jax.nn.softmax(jnp.where(m_c, s_c, NEG), axis=-1) * m_c
    o_cmp = jnp.einsum('bsghn,bngd->bsghd', p_c.astype(vc.dtype), vc)

    n_sel = S // SEL_BLOCK
    top = min(SEL_TOPK, n_sel)
    sel_start = jnp.arange(n_sel, dtype=jnp.int32) * SEL_BLOCK
    overlap = jnp.clip(
        jnp.minimum(starts[:, None] + CMP_BLOCK, sel_start[None, :] + SEL_BLOCK)
        - jnp.maximum(starts[:, None], sel_start[None, :]), 0, None
    ).astype(jnp.float32) / CMP_BLOCK
    imp = jnp.einsum('bsgn,nj->bsgj', jnp.sum(p_c, axis=3), overlap)
    cur = pos // SEL_BLOCK
    blk = jnp.arange(n_sel, dtype=jnp.int32)
    forced = (blk[None, :] == 0) | (blk[None, :] == cur[:, None]) | (blk[None, :] == cur[:, None] - 1)
    valid = blk[None, :] <= cur[:, None]
    imp = jnp.where(forced[None, :, None, :], FORCE,
                    jnp.where(valid[None, :, None, :], imp, -FORCE))
    _, sel_idx = lax.top_k(imp, top)
    sel_idx = sel_idx.transpose(0, 2, 1, 3)

    ks = _rope(k_sel, cos, sin).reshape(B, n_sel, SEL_BLOCK, G, HEAD_DIM).transpose(0, 3, 1, 2, 4)
    vs = v_sel.reshape(B, n_sel, SEL_BLOCK, G, HEAD_DIM).transpose(0, 3, 1, 2, 4)
    pad = ((0, 0), (WINDOW, 0), (0, 0), (0, 0))
    kw = jnp.pad(_rope(k_win, cos, sin), pad)
    vw = jnp.pad(v_win, pad)
    bi = jnp.arange(B)[:, None, None, None]
    gi = jnp.arange(G)[None, :, None, None]
    jj = jnp.arange(SEL_BLOCK, dtype=jnp.int32)
    wj = jnp.arange(Q_BLOCK + WINDOW, dtype=jnp.int32)

    def block(qb):
        q0 = qb * Q_BLOCK
        qq = lax.dynamic_slice_in_dim(qr, q0, Q_BLOCK, axis=1)
        tq = q0 + jnp.arange(Q_BLOCK, dtype=jnp.int32)
        idx = lax.dynamic_slice_in_dim(sel_idx, q0, Q_BLOCK, axis=2)
        kg = ks[bi, gi, idx]
        vg = vs[bi, gi, idx]
        s = jnp.einsum('bqghd,bgqnjd->bgqhnj', qq, kg).astype(jnp.float32) * scale
        kpos = idx[..., None] * SEL_BLOCK + jj
        m = (kpos <= tq[None, None, :, None, None])[:, :, :, None]
        s = jnp.where(m, s, NEG).reshape(B, G, Q_BLOCK, HG, top * SEL_BLOCK)
        p = jax.nn.softmax(s, axis=-1).reshape(B, G, Q_BLOCK, HG, top, SEL_BLOCK)
        o_s = jnp.einsum('bgqhnj,bgqnjd->bqghd', p.astype(vg.dtype), vg)
        kk = lax.dynamic_slice_in_dim(kw, q0, Q_BLOCK + WINDOW, axis=1)
        vv = lax.dynamic_slice_in_dim(vw, q0, Q_BLOCK + WINDOW, axis=1)
        kp = q0 - WINDOW + wj
        d = tq[:, None] - kp[None, :]
        mw = ((d >= 0) & (d < WINDOW) & (kp[None, :] >= 0))[None, :, None, None, :]
        sw = jnp.einsum('bqghd,bkgd->bqghk', qq, kk).astype(jnp.float32) * scale
        pw = jax.nn.softmax(jnp.where(mw, sw, NEG), axis=-1)
        o_w = jnp.einsum('bqghk,bkgd->bqghd', pw.astype(vv.dtype), vv)
        return o_s, o_w

    o_sel, o_win = lax.map(block, jnp.arange(S // Q_BLOCK, dtype=jnp.int32))
    o_sel = o_sel.transpose(1, 0, 2, 3, 4, 5).reshape(B, S, G, HG, HEAD_DIM)
    o_win = o_win.transpose(1, 0, 2, 3, 4, 5).reshape(B, S, G, HG, HEAD_DIM)
    g = gates.reshape(B, S, G, HG, 3)
    o = g[..., 0:1] * o_cmp + g[..., 1:2] * o_sel + g[..., 2:3] * o_win
    return o.reshape(B, S, NSA_WIDTH)

def _gmlp(uv, ln_g, ln_b, ws, bs):
    B, S = uv.shape[0], uv.shape[1]
    u, v = jnp.split(jax.nn.gelu(uv), 2, axis=-1)
    v = _layernorm(v, ln_g, ln_b)
    v = v.reshape(B, S // GM_CHUNK, GM_CHUNK, GM_GROUPS, HEAD_DIM)
    w = ws * jnp.tril(jnp.ones((GM_CHUNK, GM_CHUNK), ws.dtype))
    sv = jnp.einsum('gts,bnsgc->bntgc', w, v) + bs.T[None, None, :, :, None]
    return u * sv.reshape(B, S, GM_WIDTH)

def second_inputs(seed: int = 0) -> dict:
    key = jax.random.key(seed)
    k = jax.random.split(key, 24)
    L, D = DEPTH, D_MODEL

    def nrm(kk, shape, scale):
        return jax.random.normal(kk, shape, jnp.float32) * scale

    return {
        "x": nrm(k[0], (BATCH, SEQ, D), 1.0),
        "c": nrm(k[1], (BATCH, D), 1.0),
        "ada_w": nrm(k[2], (L, D, 9 * D), 0.5 * D ** -0.5),
        "ada_b": nrm(k[3], (L, 9 * D), 0.1),
        "norm_g": 1.0 + nrm(k[4], (L, 3, D), 0.1),
        "ffn_w_in": nrm(k[5], (L, 2, D, 2 * D_FF), D ** -0.5),
        "ffn_w_out": nrm(k[6], (L, 2, D_FF, D), D_FF ** -0.5),
        "mix_w_in": nrm(k[7], (L, D, IN_WIDTH), D ** -0.5),
        "cmp_pe": nrm(k[8], (L, 2, CMP_BLOCK, HEAD_DIM), 0.1),
        "cmp_w1": nrm(k[9], (L, 2, CMP_BLOCK, HEAD_DIM, CMP_HIDDEN), (CMP_BLOCK * HEAD_DIM) ** -0.5),
        "cmp_w2": nrm(k[10], (L, 2, CMP_HIDDEN, HEAD_DIM), CMP_HIDDEN ** -0.5),
        "gm_ln_g": 1.0 + nrm(k[11], (L, GM_WIDTH), 0.1),
        "gm_ln_b": nrm(k[12], (L, GM_WIDTH), 0.1),
        "gm_ws": nrm(k[13], (L, GM_GROUPS, GM_CHUNK, GM_CHUNK), GM_CHUNK ** -0.5),
        "gm_bs": 1.0 + nrm(k[14], (L, GM_GROUPS, GM_CHUNK), 0.1),
        "proj_a": nrm(k[15], (L, NSA_WIDTH, D), NSA_WIDTH ** -0.5),
        "proj_b": nrm(k[16], (L, GM_WIDTH, D), GM_WIDTH ** -0.5),
        "w_out": nrm(k[17], (L, D, D), D ** -0.5),
        "final_g": 1.0 + nrm(k[18], (D,), 0.1),
    }

def second_block(x, c, ada_w, ada_b, norm_g, ffn_w_in, ffn_w_out, mix_w_in, cmp_pe, cmp_w1,
              cmp_w2, gm_ln_g, gm_ln_b, gm_ws, gm_bs, proj_a, proj_b, w_out, final_g):
    B, S, D = x.shape
    h = x
    for l in range(DEPTH):
        mod = (jax.nn.silu(c) @ ada_w[l] + ada_b[l]).reshape(B, 3, 3, 1, D)

        n = _modulate(_rmsnorm(h, norm_g[l, 0]), mod[:, 0, 0], mod[:, 0, 1])
        h = h + 0.5 * mod[:, 0, 2] * _swiglu(n, ffn_w_in[l, 0], ffn_w_out[l, 0])

        n = _modulate(_rmsnorm(h, norm_g[l, 1]), mod[:, 1, 0], mod[:, 1, 1])
        z = n @ mix_w_in[l]
        zq, zkv, zg, zuv, zga, zgb = jnp.split(z, IN_SPLITS, axis=-1)
        q = zq.reshape(B, S, NSA_HEADS, HEAD_DIM)
        kv = zkv.reshape(B, S, 6, NSA_KV_GROUPS, HEAD_DIM)
        nsa_gates = jax.nn.sigmoid(zg).reshape(B, S, NSA_HEADS, 3)
        y_a = _nsa(q, kv[:, :, 0], kv[:, :, 1], kv[:, :, 2], kv[:, :, 3], kv[:, :, 4], kv[:, :, 5],
                   nsa_gates, cmp_pe[l], cmp_w1[l], cmp_w2[l])
        y_b = _gmlp(zuv, gm_ln_g[l], gm_ln_b[l], gm_ws[l], gm_bs[l])
        merged = jax.nn.sigmoid(zga) * (y_a @ proj_a[l]) + jax.nn.sigmoid(zgb) * (y_b @ proj_b[l])
        h = h + mod[:, 1, 2] * (merged @ w_out[l])

        n = _modulate(_rmsnorm(h, norm_g[l, 2]), mod[:, 2, 0], mod[:, 2, 1])
        h = h + 0.5 * mod[:, 2, 2] * _swiglu(n, ffn_w_in[l, 1], ffn_w_out[l, 1])
    return _rmsnorm(h, final_g)


def setup_inputs(seed=0):
    out = dict(first_inputs(seed))
    for name, value in second_inputs(seed + 1).items():
        if name != "x":
            out[name + "_2"] = value
    return out


def reference(
    x, c, positions, ada_w, ada_b, norm_g, ffn_wi, ffn_wo, a_w_in, a_w_out, a_lb, a_onorm,
    b_w_in, b_w_out, b_qk_g, b_lam, b_subln, c_w_in, c_conv, c_w_out, c_2, ada_w_2, ada_b_2,
    norm_g_2, ffn_w_in_2, ffn_w_out_2, mix_w_in_2, cmp_pe_2, cmp_w1_2, cmp_w2_2, gm_ln_g_2,
    gm_ln_b_2, gm_ws_2, gm_bs_2, proj_a_2, proj_b_2, w_out_2, final_g_2,
):
    x = first_block(
        x, c, positions, ada_w, ada_b, norm_g, ffn_wi, ffn_wo, a_w_in, a_w_out, a_lb, a_onorm,
        b_w_in, b_w_out, b_qk_g, b_lam, b_subln, c_w_in, c_conv, c_w_out,
    )
    return second_block(
        x, c_2, ada_w_2, ada_b_2, norm_g_2, ffn_w_in_2, ffn_w_out_2, mix_w_in_2, cmp_pe_2,
        cmp_w1_2, cmp_w2_2, gm_ln_g_2, gm_ln_b_2, gm_ws_2, gm_bs_2, proj_a_2, proj_b_2, w_out_2,
        final_g_2,
    )


_drawn_inputs = setup_inputs


def setup_inputs(seed=0):
    import zlib

    import numpy as np

    out = dict(_drawn_inputs(seed))
    spreads = {}
    factors = {'a_onorm': 4.339,
     'b_qk_g': 5.111,
     'b_subln': 54.256,
     'cmp_pe_2': 52.242,
     'gm_ln_g_2': 61.268,
     'gm_ln_b_2': 69.567,
     'gm_bs_2': 46.308,
     'cmp_w1_2': 3.975,
     'cmp_w2_2': 3.597,
     'ffn_w_in_2': 3.253,
     'ffn_w_out_2': 3.278}
    for name, (base, spread) in spreads.items():
        noise = np.random.default_rng([zlib.crc32(name.encode()), seed]).standard_normal(out[name].shape)
        drawn = base * np.exp(spread * noise) if base else spread * noise
        out[name] = __import__('jax').numpy.asarray(drawn.astype(out[name].dtype))
    for name, factor in factors.items():
        out[name] = (out[name] * factor).astype(out[name].dtype)
    return out
```

```python
import math
from contextlib import ExitStack

import concourse.bass as bass
from concourse import mybir

F32 = mybir.dt.float32
F32R = mybir.dt.float32r
I32 = mybir.dt.int32
ACT = mybir.ActivationFunctionType
ALU = mybir.AluOpType
AX = mybir.AxisListType.X

P = 128
S = 256
NT = S // P
D = 1024
ND = D // P
F = 2816
CF = 256
NF = F // CF
PIECE = 2048
RING = 3
ADA_RING = 2
ARENA = 13312
MODS = 9 * ND
EPS = 1e-6
NEG = -1e30
NCMP = (S - 32) // 16 + 1
LAMBDA_INIT = 0.8 - 0.6 * math.exp(-0.3)
TWO_PI = 2.0 * math.pi
PI_A = 6.28125
PI_B = math.floor((TWO_PI - PI_A) * 2 ** 19) / 2 ** 19
PI_C = TWO_PI - PI_A - PI_B

C_ID = 0
C_CAUSAL = C_ID + P
C_TRIL = C_CAUSAL + P
C_SCAN = C_TRIL + P
NLEVEL = 7
C_LEVEL = C_SCAN + 4 * S
C_CMPM = C_LEVEL + NLEVEL * P
C_CMPN = C_CMPM + NT * NCMP
C_COS = C_CMPN + NT * NCMP
C_SIN = C_COS + NT * 32
C_CCOS = C_SIN + NT * 32
C_CSIN = C_CCOS + 32
C_FREQ = C_CSIN + 32
C_END = C_FREQ + 8
N_CONST = 14


class Tally:

    def __init__(self, **credits):
        self.n, self.i, self.per = dict(credits), None, {}

    def next(self, sem, by=1):
        name = label(sem)
        self.n[name] = self.n.get(name, 0) + by
        per = self.per.get(name, 0) if self.i is not None else 0
        return self.i * per + self.n[name] if per else self.n[name]

    def enter(self, i, per):
        self.i, self.per, self.before = i, {label(s): k for s, k in per}, dict(self.n)

    def leave(self, turns):
        for name in self.n:
            before, per = self.before.get(name, 0), self.per.get(name, 0)
            assert self.n[name] - before == per, (name, self.n[name] - before, per)
            self.n[name] = before + turns * per
        self.i, self.per = None, {}


def label(sem):
    return sem if isinstance(sem, str) else sem.name


def bc(ap, shape):
    return ap.broadcast_to(shape)


def build(nc, T, out, upto=99):
    with ExitStack() as ctx:
        def sb(name, shape, dt=F32):
            return ctx.enter_context(nc.sbuf_tensor(name, shape, dt))

        def sem(name):
            return ctx.enter_context(nc.semaphore(name))

        PY = ctx.enter_context(nc.psum_tensor("PY", [P, 4, 512], F32))
        GU = ctx.enter_context(nc.psum_tensor("GU", [P, 2, 512], F32))
        TM = ctx.enter_context(nc.psum_tensor("TM", [P, 2, 512], F32))
        PYt = PY[:, :, :].rearrange("p b (d s) -> p (b d) s", d=2)

        raw = sb("raw", [P, RING, PIECE])
        wH = sb("wH", [P, RING, PIECE], F32R)
        wL = sb("wL", [P, RING, PIECE], F32R)
        ada = sb("ada", [P, ADA_RING, PIECE])
        acc = sb("acc", [P, 512])
        x = sb("x", [P, NT, D])
        xn = sb("xn", [P, NT, D])
        xH = sb("xH", [P, ND, S], F32R)
        xL = sb("xL", [P, ND, S], F32R)
        hH = sb("hH", [P, 2, S], F32R)
        hL = sb("hL", [P, 2, S], F32R)
        sh = sb("sh", [P, 2, NT, CF])
        gB = sb("gB", [P, D])
        cst = sb("cst", [P, C_END])
        rows = sb("rows", [P, 6, P])
        cols = sb("cols", [P, P])
        bT = sb("bT", [P, 4 * MODS])
        mod = sb("mod", [P, 4 * MODS])
        cs = sb("cs", [P, 2 * ND])
        vb = sb("vb", [P, 5 * P])
        posi = sb("posi", [P, NT], I32)
        posf = sb("posf", [P, NT])
        turns_i = sb("turns_i", [P, NT, 8], I32)
        turns_f = sb("turns_f", [P, NT, 8])
        ang = sb("ang", [P, 2, NT, 8])
        wrap = sb("wrap", [P, 2, NT, 8])
        lam = sb("lam", [P, 8])
        ones = sb("ones", [P, 1])
        st = sb("st", [P, 8])
        scl = sb("scl", [P, ND])
        gcol = sb("gcol", [P, ND])
        M = sb("M", [P, ARENA])
        modf = M[:, 0:2 * D].rearrange("p (b n) -> p b n", b=4)
        xH2 = xH[:, :, :].rearrange("p (b d) s -> p b (d s)", d=2)
        xL2 = xL[:, :, :].rearrange("p (b d) s -> p b (d s)", d=2)
        ident = cst[:, C_ID:C_ID + P]
        shf = sh[:, :, :, :].rearrange("p a t f -> p (a t f)")

        k_, q_, b_ = (M[:, n * D:(n + 1) * D] for n in range(3))
        E = [M[:, n * D:(n + 1) * D] for n in (3, 4, 5)]
        att = M[:, 6 * D:7 * D].rearrange("p (h s) -> p h s", s=P)
        attX = M[:, 7 * D:7 * D + 512].rearrange("p (h s) -> p h s", s=P)
        v_ = M[:, 7 * D + 512:9 * D + 512].rearrange("p (t n) -> p t n", t=NT)
        g_ = M[:, 9 * D + 512:11 * D + 512].rearrange("p (t n) -> p t n", t=NT)
        qk_, sq_ = M[:, 0:D], M[:, D:2 * D]
        qT = M[:, 2 * D:4 * D].rearrange("p (h s) -> p h s", s=S)
        kT = M[:, 4 * D:6 * D].rearrange("p (h s) -> p h s", s=S)
        vB = M[:, 6 * D:8 * D].rearrange("p (t n) -> p t n", t=NT)
        p_ = [M[:, n * D:(n + 1) * D].rearrange("p (m s) -> p m s", s=S) for n in (8, 9)]
        a_ = [M[:, (20 + n) * 512:(21 + n) * 512].rearrange("p (h s) -> p h s", s=S) for n in range(2)]
        aT = [M[:, (22 + n) * 512:(23 + n) * 512] for n in range(2)]
        rot = M[:, 24 * 512:25 * 512].rearrange("p (n t g d) -> p n t g d", n=4, t=NT, g=8)
        on_ = [M[:, n * D:(n + 1) * D] for n in range(NT)]
        v2_ = M[:, 0:512].rearrange("p (b t n) -> p b t n", b=2, t=NT)
        qT2 = M[:, 512:1536].rearrange("p (h s) -> p h s", s=S)
        kT2 = M[:, 1536:2560].rearrange("p (b g s) -> p b g s", b=2, g=2)
        kcT = M[:, 2560:2592].rearrange("p (g n) -> p g n", g=2)
        vc_ = M[:, 2592:2720].rearrange("p (g n) -> p g n", g=2)
        gates = M[:, 2720:2768].rearrange("p (t h c b) -> p t h c b", t=NT, h=4, c=2)
        pc_ = M[:, 2768:3008].rearrange("p (c m n) -> p c m n", c=2, n=NCMP)
        pcf = M[:, 2768:3008].rearrange("p (m n) -> p m n", n=NCMP)
        kd_ = M[:, 3072:4096].rearrange("p (b t g c n) -> p b t g c n", b=2, t=NT, g=2, c=2)
        cT_ = M[:, 4096:5120].rearrange("p (j g s) -> p j g s", j=2, g=2)
        w1_ = [M[:, 5120:7168], M[:, 8192:10240]]
        rt_ = M[:, 7168:8192]
        a2_ = [M[:, n:n + D].rearrange("p (m s) -> p m s", s=S) for n in (3072, 4096)]
        aT2 = [M[:, n:n + D] for n in (5120, 6144)]
        yo_ = M[:, 7168:8192].rearrange("p (t n) -> p t n", t=NT)
        u_ = M[:, 8192:9216].rearrange("p (t n) -> p t n", t=NT)
        vg_ = M[:, 9216:10240].rearrange("p (t n) -> p t n", t=NT)
        ws_ = M[:, 10240:11264].rearrange("p (g s) -> p g s", s=P)
        wsT = M[:, 11264:12288]
        ln_ = M[:, 12288:13312].rearrange("p (a n) -> p a n", a=2)
        cd_ = xn[:, 0, :].rearrange("p (t m c n) -> p t m c n", t=NT, m=4, c=2)
        qr_ = xn[:, 1, :].rearrange("p (t n) -> p t n", t=NT)
        y_ = shf.rearrange("p (t n) -> p t n", t=NT)
        sg_ = [ada[:, n, :].rearrange("p (t n) -> p t n", t=NT) for n in range(2)]
        w2_ = sb("w2_", [P, 2, 64])
        peT = sb("peT", [P, 64])
        pec = sb("pec", [P, 2])
        hc_ = sb("hc_", [P, 2, 30])
        kct = rt_[:, 0:256].rearrange("p (n g d) -> p n g d", n=4, g=2)
        kcd = rt_[:, 256:512].rearrange("p (g c n) -> p g c n", g=2, c=2)
        bn_ = sb("bn_", [P, NT, 6])
        mv_ = sb("mv_", [P, NT, 2])
        C_ = lambda at, n: cst[:, at:at + n]
        cos2 = C_(C_COS, NT * 32).rearrange("p (t n) -> p t n", t=NT)
        sin2 = C_(C_SIN, NT * 32).rearrange("p (t n) -> p t n", t=NT)
        stu = sb("stu", [P, 2, 16])
        causal = cst[:, C_CAUSAL:C_CAUSAL + P]
        st8 = sb("st8", [P, 4, 32])
        GUf = GU[:, :, :].rearrange("p b n -> p (b n)")
        PAf = PY[:, 0:2, :].rearrange("p b n -> p (b n)")
        PBf = PY[:, 2:4, :].rearrange("p b n -> p (b n)")
        TMf = TM[:, :, :].rearrange("p b n -> p (b n)")

        s_const = sem("s_const")
        s_ones = sem("s_ones")
        s_raw = [sem(f"s_raw{i}") for i in range(RING)]
        s_high = sem("s_high")
        s_split = sem("s_split")
        s_eaten = sem("s_eaten")
        s_ada = [sem(f"s_ada{i}") for i in range(ADA_RING)]
        s_adafree = sem("s_adafree")
        s_acc = sem("s_acc")
        s_modp = sem("s_modp")
        s_dve = sem("s_dve")
        s_act = sem("s_act")
        s_col = sem("s_col")
        s_cs = sem("s_cs")
        s_x = sem("s_x")
        s_ss = sem("s_ss")
        s_var = sem("s_var")
        s_sd = sem("s_sd")
        s_xn = sem("s_xn")
        s_xt = sem("s_xt")
        s_modf0 = sem("s_modf0")
        s_modf1 = sem("s_modf1")
        s_xh = sem("s_xh")
        s_xl = sem("s_xl")
        s_scl = sem("s_scl")
        s_gcol = sem("s_gcol")
        s_gp = sem("s_gp")
        s_gb = sem("s_gb")
        s_silu = sem("s_silu")
        s_h = sem("s_h")
        s_ht = sem("s_ht")
        s_hh = sem("s_hh")
        s_hl = sem("s_hl")
        s_out = sem("s_out")
        s_readA = sem("s_readA")
        s_readD = sem("s_readD")
        s_key = sem("s_key")
        s_sigq = sem("s_sigq")
        s_ln = sem("s_ln")
        s_expo = sem("s_expo")
        s_decay = sem("s_decay")
        s_z = sem("s_z")
        s_gram = sem("s_gram")
        s_sel = sem("s_sel")
        s_o = sem("s_o")
        s_sq = sem("s_sq")
        s_hvar = sem("s_hvar")
        s_hsd = sem("s_hsd")
        s_w1 = sem("s_w1")
        s_gm = sem("s_gm")
        s_gate = sem("s_gate")
        s_cmp = sem("s_cmp")
        s_hc = sem("s_hc")
        s_kc = sem("s_kc")
        s_wm = sem("s_wm")
        s_bnv = sem("s_bnv")
        s_bns = sem("s_bns")
        s_vn = sem("s_vn")
        s_sv = sem("s_sv")
        s_yb = sem("s_yb")
        s_cx = sem("s_cx")
        s_ce = sem("s_ce")
        s_pc = sem("s_pc")
        s_trig = sem("s_trig")
        s_trigd = sem("s_trigd")
        s_score = sem("s_score")
        s_scored = sem("s_scored")
        s_max = sem("s_max")
        s_exp = sem("s_exp")
        s_a = sem("s_a")
        s_at = sem("s_at")
        s_aT = sem("s_aT")
        s_merged = sem("s_merged")
        s_on = sem("s_on")
        s_ot = sem("s_ot")

        ONE = dict(ada="ada_w", wi="ffn_wi", wo="ffn_wo")
        TWO = dict(ada="ada_w_2", wi="ffn_w_in_2", wo="ffn_w_out_2")
        LAYERS = [(ONE, 0), (ONE, 1), (TWO, 0), (TWO, 1)]
        ADA_FIRST, ADA_REST = 8, 10

        PHASES = [(l, j) for l in range(4) for j in range(3)][:upto]
        PIECES = [20, 16, 26, 26]


        def ada_turns(l, j):
            if j == 0:
                return l, ADA_FIRST, ADA_REST
            return (l + 1, 0, ADA_FIRST) if l + 1 < len(LAYERS) else (l, 0, 0)

        MIX_CHUNKS = [(512, 512), (0, 512), (1024, 280), (1816, 512), (1304, 512), (2328, 512), (2840, 512),
                      (3352, 512), (3864, 512)]

        block = ctx.enter_context(nc.Block())

        @block.sync
        def _(sp):
            t = Tally()

            def load(view, k0, nk, lo, width):
                slot = t.next("piece") % RING
                sp.wait_ge(s_split, t.next(s_split))
                dst = raw[:, slot, 0:nk * width].rearrange("p (k n) -> p k n", k=nk)
                for q in range(2):
                    sp.dma_start(dst[:, q * nk // 2:(q + 1) * nk // 2, :],
                                 view[:, k0 + q * nk // 2:k0 + (q + 1) * nk // 2, lo:lo + width]
                                 ).then_inc(s_raw[slot], 16)

            def load_up(l, j, c, q):
                names, i = LAYERS[l]
                v = T[names["wi"]][i, j // 2].rearrange("(k p) (two f) -> p k two f", p=P, two=2)
                slot = t.next("piece") % RING
                sp.wait_ge(s_split, t.next(s_split))
                dst = raw[:, slot, :].rearrange("p (k two f) -> p k two f", k=4, two=2)
                for g in range(2):
                    sp.dma_start(dst[:, :, g, :], v[:, 4 * q:4 * q + 4, g, bass.ds(c * CF, CF)]
                                 ).then_inc(s_raw[slot], 16)

            def load_down(l, j, c):
                names, i = LAYERS[l]
                v = T[names["wo"]][i, j // 2].rearrange("(c k p) n -> c p k n", p=P, k=2)
                slot = t.next("piece") % RING
                sp.wait_ge(s_split, t.next(s_split))
                dst = raw[:, slot, :].rearrange("p (k n) -> p k n", k=2)
                for k in range(2):
                    sp.dma_start(dst[:, k, :], v[bass.ds(c, 1), :, k, :].rearrange("c p n -> p (c n)")
                                 ).then_inc(s_raw[slot], 16)

            def load_ada(l, c, q):
                names, i = LAYERS[l]
                v = T[names["ada"]][i].rearrange("(k p) n -> p k n", p=P)
                slot = t.next("ada") % ADA_RING
                sp.wait_ge(s_adafree, t.next(s_adafree))
                sp.dma_start(ada[:, slot, :].rearrange("p (k n) -> p k n", k=4),
                             v[:, 4 * q:4 * q + 4, bass.ds(c * 512, 512)]).then_inc(s_ada[slot], 16)

            def ffn(l, j):
                load_up(l, j, 0, 0)
                load_up(l, j, 0, 1)
                la, c0, turns = ada_turns(l, j)

                def loop(first, count, with_ada):
                    with sp.Fori(0, count) as i:
                        t.enter(i, [(s_split, 3), ("piece", 3), (s_adafree, 2 * with_ada), ("ada", 2 * with_ada)])
                        load_up(l, j, first + i, 0)
                        if with_ada:
                            load_ada(la, c0 + i, 0)
                        load_up(l, j, first + i, 1)
                        if with_ada:
                            load_ada(la, c0 + i, 1)
                        load_down(l, j, first + i - 1)
                    t.leave(count)

                if turns:
                    if l == 2 and j == 2:
                        sp.wait_ge(s_x, 3 * l + 2)
                    loop(1, turns, 1)
                if turns < NF - 1:
                    loop(1 + turns, NF - 1 - turns, 0)
                load_down(l, j, NF - 1)

            sp.dma_start(rows[0:16, 0, :], T["vec_rows"][0:16, :]).then_inc(s_const, 16)
            sp.dma_start(cst[:, :], T["table"]).then_inc(s_const, 16)
            sp.dma_start(rows[16:P, 0, :], T["vec_rows"][16:P, :]).then_inc(s_const, 16)
            sp.dma_start(rows[0:64, 5, :], T["cmp_pe_2"].rearrange("l j (k two) d -> (l j k) (two d)", two=2)
                         ).then_inc(s_const, 16)
            sp.dma_start(posi[:, :], T["positions"][0].rearrange("(t p) -> p t", p=P),
                         allow_slow_non_contiguous=True).then_inc(s_const, 16)
            for at, n, name in ((0, P, "a_onorm"), (P, P, "b_qk_g"), (2 * P, P, "b_subln"), (3 * P, 2 * P, "b_lam")):
                sp.dma_start(vb[:, at:at + n], T[name].rearrange(
                    "a n -> (a n)" if len(T[name].shape) == 2 else "a b n -> (a b n)").unsqueeze(0).broadcast_to([P, n])
                    ).then_inc(s_const, 16)
            for l in range(4):
                sp.dma_start(rows[0:MODS, 1 + l, :], T["ada_b" if l < 2 else "ada_b_2"][l % 2].rearrange(
                    "(r n) -> r n", n=P)).then_inc(s_const, 16)
            sp.dma_start(x[:, :, :], T["x"][0].rearrange("(t p) d -> p t d", p=P)).then_inc(s_const, 16)
            for c in range(ADA_FIRST):
                for q in range(2):
                    load_ada(0, c, q)
            for l, j in PHASES:
                if j != 1:
                    ffn(l, j)
                elif l == 0:
                    w = T["a_w_in"][0].rearrange("(k p) n -> p k n", p=P)
                    for lo in (D, 0, 2 * D, 2 * D + 512, 3 * D, 3 * D + 512, D + 512, 512):
                        load(w, 0, 4, lo, 512)
                        load(w, 4, 4, lo, 512)
                    w = T["a_w_out"][0].rearrange("(k p) n -> p k n", p=P)
                    for lo in (0, 512):
                        load(w, 0, 4, lo, 512)
                        load(w, 4, 4, lo, 512)
                elif l == 1:
                    for name, halves in (("b_w_in", 6), ("b_w_out", 2)):
                        w = T[name][0].rearrange("(k p) n -> p k n", p=P)
                        for h in range(halves):
                            load(w, 0, 4, h * 512, 512)
                            load(w, 4, 4, h * 512, 512)
                else:
                    i = l - 2
                    sp.wait_ge(s_x, 3 * l - 1)
                    for k in range(2):
                        for two in range(2):
                            sp.dma_start(w1_[k].rearrange("p (l f) -> p l f", f=P)[two * 64:(two + 1) * 64],
                                         T["cmp_w1_2"][i, k].rearrange("(l two) d f -> two d l f", two=2)[two]
                                         ).then_inc(s_w1, 16)
                    sp.dma_start(w2_[:, :, :], T["cmp_w2_2"][i].rearrange("j f d -> f j d")).then_inc(s_w1, 16)
                    sp.dma_start(ws_, T["gm_ws_2"][i].rearrange("g t s -> t g s")).then_inc(s_gm, 16)
                    for k, name in enumerate(("gm_ln_g_2", "gm_ln_b_2")):
                        sp.dma_start(ln_[:, k, :], T[name][i].unsqueeze(0).broadcast_to([P, 512])).then_inc(s_gm, 16)
                    w = T["mix_w_in_2"][i].rearrange("(k p) n -> p k n", p=P)
                    for lo, width in MIX_CHUNKS:
                        load(w, 0, 4, lo, width)
                        load(w, 4, 4, lo, width)
                    for h in range(2):
                        for name in ("proj_a_2", "proj_b_2"):
                            load(T[name][i].rearrange("(k p) n -> p k n", p=P), 0, 4, h * 512, 512)
                    w = T["w_out_2"][i].rearrange("(k p) n -> p k n", p=P)
                    for h in range(2):
                        load(w, 0, 4, h * 512, 512)
                        load(w, 4, 4, h * 512, 512)
            if len(PHASES) == 12:
                sp.wait_ge(s_x, 11)
                sp.dma_start(ln_, T["final_g_2"].unsqueeze(0).broadcast_to([P, D])
                             .rearrange("p (a n) -> p a n", a=2)).then_inc(s_const, 16)
            sp.wait_ge(s_x, len(PHASES) + (len(PHASES) == 12))
            sp.dma_start(out[0].rearrange("(t p) d -> p t d", p=P), x[:, :, :]).then_inc(s_out, 16)
            sp.wait_ge(s_out, 16)

        @block.scalar
        def _(act):
            t = Tally(done=RING)

            def cut(words=PIECE):
                slot = t.next("piece") % RING
                act.wait_ge(s_raw[slot], t.next(s_raw[slot], 32))
                act.wait_ge(s_eaten, t.next(s_eaten))
                act.activation(wH[:, slot, 0:words], raw[:, slot, 0:words], ACT.Copy).then_inc(s_high, 1)

            def squares_and_roots(first=False):
                if not first:
                    act.wait_ge(s_x, t.next(s_x))
                for i in range(NT):
                    act.activation(xn[:, i, :], x[:, i, :], ACT.Square, accum_out=st[:, i:i + 1]).then_inc(s_ss, 1)
                act.wait_ge(s_var, t.next(s_var))
                act.activation(st[:, 4:6], st[:, 2:4], ACT.Sqrt).then_inc(s_sd, 1)

            def norm(l, j):
                squares_and_roots((l, j) == PHASES[0])
                act.wait_ge(s_gp, t.next(s_gp))
                act.activation(gB[:, :], TM[:, :, :].rearrange("p b n -> p (b n)"), ACT.Copy).then_inc(s_gb, 1)
                act.wait_ge(s_scl, t.next(s_scl))
                m = (3 * l + j) * 3 * ND
                for b in (1, 3):
                    act.wait_ge(s_xt, t.next(s_xt, 2))
                    for d in (2 * b, 2 * b + 1):
                        ins = act.activation(modf[:, b, (d % 2) * S:(d % 2 + 1) * S], PYt[:, d, :], ACT.Identity,
                                             bias=mod[:, m + d:m + d + 1], scale=scl[:, d:d + 1])
                    ins.then_inc(s_modf1, 1)
                    act.wait_ge(s_modf0, t.next(s_modf0))
                    act.activation(xH2[:, b - 1, :], modf[:, b - 1, :], ACT.Copy).then_inc(s_xh, 1)
                    act.wait_ge(s_modf1, t.next(s_modf1))
                    act.activation(xH2[:, b, :], modf[:, b, :], ACT.Copy).then_inc(s_xh, 1)

            def silu_gate():
                act.wait_ge(s_eaten, t.next("done", 2))
                act.activation(sh[:, 0, :, :], GU[:, :, 0:CF], ACT.Silu).then_inc(s_silu, 1)

            def hidden_high():
                act.wait_ge(s_ht, t.next(s_ht))
                act.activation(hH[:, :, :].rearrange("p f s -> p (f s)"), TM[:, 0, :], ACT.Copy).then_inc(s_hh, 1)

            def ffn(l, j):
                norm(l, j)
                silu_gate()

                def loop(count):
                    with act.Fori(0, count) as i:
                        t.enter(i, [("piece", 3), (s_eaten, 3), ("done", 3), (s_ht, 1)] + [(s, 32) for s in s_raw])
                        cut()
                        cut()
                        hidden_high()
                        cut()
                        silu_gate()
                        t.next("done")
                    t.leave(count)

                _, _, turns = ada_turns(l, j)
                if turns:
                    loop(turns)
                if turns < NF - 1:
                    loop(NF - 1 - turns)
                hidden_high()
                cut()
                t.next("done")

            def head_norm(src, dst):
                act.wait_ge(s_o, t.next(s_o))
                act.activation(dst, src, ACT.Square).then_inc(s_sq, 1)

            def head_root(n):
                act.wait_ge(s_hvar, t.next(s_hvar))
                act.activation(st8[:, 1, 0:n], st8[:, 0, 0:n], ACT.Sqrt).then_inc(s_hsd, 1)

            def evacuate(dst, src, func=ACT.Copy):
                act.wait_ge(s_eaten, t.next("done", 2))
                act.activation(dst, src, func).then_inc(s_readA, 1)

            def chained(instruction):
                instruction.then_inc(s_act, 1)
                act.wait_ge(s_act, t.next(s_act))

            def high_out(dst, src):
                act.wait_ge(s_ot, t.next(s_ot))
                act.activation(dst, src, ACT.Copy).then_inc(s_xh, 1)

            def hgrn():
                norm(0, 1)
                cut()
                cut()
                for grp in range(2):
                    act.wait_ge(s_eaten, t.next("done", 2))
                    act.activation(k_, GUf, ACT.Sigmoid, scale=-1.0)
                    act.activation(E[0], GUf, ACT.Abs).then_inc(s_key, 1)
                    if grp == 0:
                        cut()
                    act.wait_ge(s_eaten, t.next("done", 2))
                    act.activation(E[1], PAf, ACT.Sigmoid).then_inc(s_sigq, 1)
                    if grp == 0:
                        cut()
                    act.wait_ge(s_key, t.next(s_key))
                    chained(act.activation(E[0], E[0], ACT.Exp, scale=-1.0))
                    act.activation(E[0], E[0], ACT.Ln, bias=1.0).then_inc(s_ln, 1)
                    if grp == 0:
                        cut()
                        cut()
                        evacuate(v_[:, :, 0:512], GU[:, :, :])
                        evacuate(v_[:, :, 512:D], PY[:, 0:2, :])
                    for n in range(9):
                        if n < 8:
                            act.wait_ge(s_expo, t.next(s_expo))
                            e = E[(n + 1) % 3]
                            act.activation(e, e, ACT.Exp).then_inc(s_decay, 1)
                        if grp == 0 and n < 8:
                            cut()
                        if grp == 0 and n == 3:
                            evacuate(g_[:, :, 0:512], GU[:, :, :], ACT.Silu)
                        if grp == 0 and n == 5:
                            evacuate(g_[:, :, 512:D], PY[:, 0:2, :], ACT.Silu)
                    head_norm(TMf, E[0])
                    head_root(8)
                    high_out(xH[:, 4 * grp:4 * grp + 4, :].rearrange("p d s -> p (d s)"), PBf)
                for _ in range(4):
                    cut()
                t.next("done", 4)

            def high_bank(b):
                act.wait_ge(s_ot, t.next(s_ot))
                act.activation(xH2[:, b, :], PY[:, b, :], ACT.Copy).then_inc(s_xh, 1)

            def exponentials(u, width):
                act.wait_ge(s_max, t.next(s_max))
                for m in range(4):
                    ins = act.activation(p_[u % 2][:, m, 0:width], p_[u % 2][:, m, 0:width], ACT.Exp,
                                         bias=stu[:, u % 2, m:m + 1], accum_out=stu[:, u % 2, 4 + m:5 + m])
                ins.then_inc(s_exp, 1)

            def weights_out(u, width):
                act.wait_ge(s_at, t.next(s_at))
                act.activation(aT[u % 2][:, 0:width], TM[:, u % 2, 0:width], ACT.Copy).then_inc(s_aT, 1)

            def diff():
                act.wait_ge(s_trig, 1)
                act.activation(lam[:, 2:4], lam[:, 0:2], ACT.Exp)
                act.activation(ang[:, :, :, :].rearrange("p a t n -> p (a t n)"),
                               ang[:, :, :, :].rearrange("p a t n -> p (a t n)"), ACT.Sin).then_inc(s_trigd, 1)
                norm(1, 1)
                cut()
                cut()
                for c in range(4):
                    banks = GUf if c % 2 == 0 else PAf
                    act.wait_ge(s_eaten, t.next("done", 2))
                    act.activation(sq_, banks, ACT.Square).then_inc(s_sq, 1)
                    head_root(16)
                    cut()
                    cut()
                    act.wait_ge(s_ot, t.next(s_ot))
                    dst = (qT if c < 2 else kT)[:, 4 * (c % 2):4 * (c % 2) + 4, :].rearrange("p h s -> p (h s)")
                    act.activation(dst, TMf, ACT.Copy).then_inc(s_aT, 1)
                evacuate(vB[:, :, 0:512], GU[:, :, :])
                evacuate(vB[:, :, 512:D], PY[:, 0:2, :])
                cut()
                cut()
                exponentials(0, P)
                for u in range(8):
                    if u < 7:
                        exponentials(u + 1, P * ((u + 1) // 4 + 1))
                    weights_out(u, S * (u // 4 + 1))
                    if u == 4:
                        head_norm(GUf, xn[:, 0, :])
                        head_root(8)
                head_norm(GUf, xn[:, 0, :])
                head_root(8)
                for b in range(4):
                    high_bank(b)
                cut()
                cut()
                t.next("done", 4)

            def turned(dst, src):
                act.wait_ge(s_ot, t.next(s_ot))
                act.activation(dst, src, ACT.Copy).then_inc(s_aT, 1)

            def nsa(l):
                norm(l, 1)
                cut()
                cut()
                cut(4 * 280)
                cut(4 * 280)
                act.wait_ge(s_ot, t.next(s_ot))
                src = TMf.rearrange("p (m s) -> p m s", s=S)
                dst = cT_.rearrange("p j g s -> p (j g) s")
                act.activation(dst[0:64], src[0:64], ACT.Copy)
                act.activation(dst[64:P, :, 0:S - 1], src[64:P, :, 1:S], ACT.Copy).then_inc(s_aT, 1)
                cut()
                cut()
                act.wait_ge(s_eaten, t.next("done", 6))
                act.activation(gates.rearrange("p t h c b -> p t (h c b)"), GU[:, :, 256:280],
                               ACT.Sigmoid).then_inc(s_gate, 1)
                turned(qT2.rearrange("p h s -> p (h s)"), TMf)
                act.wait_ge(s_cmp, t.next(s_cmp))
                t.next(s_cmp, 3)
                for k in range(2):
                    chained(act.activation(pec[:, k:k + 1], PY[:, 2, 64 * k + 32:64 * k + 33], ACT.Copy))
                    ins = act.activation(hc_[:, k, :], PY[:, 2, 64 * k:64 * k + 30], ACT.Silu, bias=pec[:, k:k + 1])
                ins.then_inc(s_hc, 1)
                cut()
                cut()
                evacuate(vg_, PY[:, 0:2, :], ACT.Gelu_apprx_tanh)
                act.wait_ge(s_bnv, t.next(s_bnv))
                act.activation(mv_[:, :, 1], mv_[:, :, 1], ACT.Sqrt).then_inc(s_bns, 1)
                turned(kT2.rearrange("p b g s -> p (b g s)"), TMf)
                cut()
                cut()
                evacuate(u_, GU[:, :, :], ACT.Gelu_apprx_tanh)
                turned(wsT, TMf)
                cut()
                cut()
                evacuate(sg_[0][:, :, 0:512], PY[:, 0:2, :], ACT.Sigmoid)
                cut()
                cut()
                evacuate(sg_[0][:, :, 512:D], GU[:, :, :], ACT.Sigmoid)
                cut()
                cut()
                evacuate(sg_[1][:, :, 0:512], PY[:, 0:2, :], ACT.Sigmoid)
                cut()
                evacuate(sg_[1][:, :, 512:D], GU[:, :, :], ACT.Sigmoid)
                cut()
                high_out(xH[:, 4:8, :].rearrange("p d s -> p (d s)"), PBf)
                act.wait_ge(s_cx, t.next(s_cx))
                act.activation(pcf, pcf, ACT.Exp).then_inc(s_ce, 1)
                for i in range(NT):
                    turned(xn[0:NCMP, i, :], TMf[0:NCMP])
                exponentials(0, P)
                for u in range(8):
                    tile = u // 4
                    if u < 7:
                        exponentials(u + 1, P * ((u + 1) // 4 + 1))
                    act.wait_ge(s_at, t.next(s_at))
                    if tile:
                        act.activation(aT2[u % 2], TMf, ACT.Copy).then_inc(s_aT, 1)
                    else:
                        act.activation(aT2[u % 2][:, 0:512], TM[:, u % 2, :], ACT.Copy).then_inc(s_aT, 1)
                    if u == 4:
                        act.wait_ge(s_o, t.next(s_o))
                        act.activation(yo_[:, 0, :], GU[:, 0, :], ACT.Copy).then_inc(s_readA, 1)
                act.wait_ge(s_o, t.next(s_o))
                act.activation(yo_[:, 1, :], GU[:, 1, :], ACT.Copy).then_inc(s_readA, 1)
                high_out(xH[:, 0:4, :].rearrange("p d s -> p (d s)"), PBf)
                cut()
                cut()
                cut()
                cut()
                for b in range(4):
                    high_bank(b)
                cut()
                cut()
                t.next("done", 8)

            act.wait_ge(s_col, 1)
            act.activation(cs[:, :], TM[:, 0, 0:2 * ND], ACT.Silu).then_inc(s_cs, 1)
            cut()
            cut()
            for n, (l, j) in enumerate(PHASES):
                if j != 1:
                    ffn(l, j)
                elif l == 0:
                    hgrn()
                elif l == 1:
                    diff()
                else:
                    nsa(l)
                if n + 1 < len(PHASES):
                    cut()
                    cut()
            if len(PHASES) == 12:
                squares_and_roots()

        @block.vector
        def _(dve):
            t = Tally(done=RING)

            def chained(instruction):
                instruction.then_inc(s_dve, 1)
                dve.wait_ge(s_dve, t.next(s_dve))

            def cut(words=PIECE):
                slot = t.next("piece") % RING
                dve.wait_ge(s_high, t.next(s_high))
                dve.tensor_tensor(wL[:, slot, 0:words], raw[:, slot, 0:words], wH[:, slot, 0:words],
                                  ALU.subtract).then_inc(s_split, 1)

            def ada_products(l, q):
                slot = t.next("ada") % ADA_RING
                dve.wait_ge(s_ada[slot], t.next(s_ada[slot], 16))
                for k in range(4):
                    w = ada[:, slot, k * 512:(k + 1) * 512]
                    c = cs[:, (l // 2) * ND + 4 * q + k:(l // 2) * ND + 4 * q + k + 1]
                    if q == 0 and k == 0:
                        ins = dve.tensor_scalar(acc[:, :], w, c, None, ALU.mult)
                    else:
                        ins = dve.scalar_tensor_tensor(acc[:, :], w, c, acc[:, :], ALU.mult, ALU.add)
                    chained(ins)
                dve.sem_inc(s_adafree, 1)
                if q == 1:
                    dve.sem_inc(s_acc, 1)

            def ada_store(l, c):
                dve.wait_ge(s_modp, t.next(s_modp))
                at = l * MODS + 4 * c
                chained(dve.tensor_tensor(mod[:, bass.ds(at, 4)], TM[:, 1, 0:4], bT[:, bass.ds(at, 4)], ALU.add))

            def tile_roots():
                dve.wait_ge(s_ss, t.next(s_ss, NT))
                dve.tensor_scalar(st[:, 2:4], st[:, 0:2], 1.0 / D, EPS, ALU.mult, ALU.add).then_inc(s_var, 1)
                dve.wait_ge(s_sd, t.next(s_sd))
                chained(dve.reciprocal(st[:, 6:8], st[:, 4:6]))

            def norm(l, j):
                m = (3 * l + j) * 3 * ND
                g = 2 * ND + (3 * l + j) * ND
                factor = 0.5 if j != 1 else 1.0
                gate = mod[:, m + 2 * ND:m + 3 * ND]
                if l < 2:
                    chained(dve.tensor_scalar(gcol[:, :], gate, 1.0, factor, ALU.add, ALU.mult))
                else:
                    chained(dve.tensor_scalar(gcol[:, :], gate, factor, None, ALU.mult))
                dve.tensor_copy(shf.rearrange("p (d n) -> p d n", n=P),
                                bc(gcol[:, :].unsqueeze(2), [P, ND, P])).then_inc(s_gcol, 1)
                dve.scalar_tensor_tensor(scl[:, :], mod[:, m + ND:m + 2 * ND], 1.0, cols[:, g:g + ND],
                                         ALU.add, ALU.mult).then_inc(s_scl, 1)
                dve.wait_ge(s_scl, t.next(s_scl))
                tile_roots()
                for i in range(NT):
                    dve.tensor_scalar(xn[:, i, :], x[:, i, :], st[:, 6 + i:7 + i], None,
                                      ALU.mult).then_inc(s_xn, 1)
                for b in (0, 2):
                    dve.wait_ge(s_xt, t.next(s_xt, 1 + b // 2))
                    for d in (2 * b, 2 * b + 1):
                        ins = dve.tensor_scalar(modf[:, b, (d % 2) * S:(d % 2 + 1) * S], PYt[:, d, :],
                                                scl[:, d:d + 1], mod[:, m + d:m + d + 1], ALU.mult, ALU.add)
                    ins.then_inc(s_modf0, 1)
                t.next(s_xt)
                for b in range(4):
                    dve.wait_ge(s_xh, t.next(s_xh))
                    dve.tensor_tensor(xL2[:, b, :], modf[:, b, :], xH2[:, b, :], ALU.subtract).then_inc(s_xl, 1)

            def hidden():
                dve.wait_ge(s_silu, t.next(s_silu))
                dve.tensor_tensor(sh[:, 1, :, :], sh[:, 0, :, :], GU[:, :, CF:2 * CF], ALU.mult).then_inc(s_h, 1)

            def hidden_low():
                dve.wait_ge(s_hh, t.next(s_hh))
                dve.tensor_tensor(hL[:, :, :].rearrange("p f s -> p (f s)"), TM[:, 0, :],
                                  hH[:, :, :].rearrange("p f s -> p (f s)"), ALU.subtract).then_inc(s_hl, 1)

            def residual(pieces):
                dve.wait_ge(s_gb, t.next(s_gb))
                dve.wait_ge(s_eaten, t.next("done", pieces))
                for i in range(NT):
                    ins = dve.tensor_tensor(xn[:, i, :], PY[:, 2 * i:2 * i + 2, :].rearrange("p b n -> p (b n)"),
                                            gB[:, :], ALU.mult)
                    if i == NT - 1:
                        chained(ins)
                dve.tensor_tensor(x[:, :, :], x[:, :, :], xn[:, :, :], ALU.add).then_inc(s_x, 1)
                dve.wait_ge(s_x, t.next(s_x))

            def ffn(l, j):
                norm(l, j)
                hidden()
                la, c0, turns = ada_turns(l, j)

                def loop(count, with_ada):
                    with dve.Fori(0, count) as i:
                        per = [("piece", 3), (s_high, 3), (s_silu, 1), (s_hh, 1)]
                        if with_ada:
                            per += [("ada", 2), (s_dve, 9), (s_modp, 1)] + [(s, 16) for s in s_ada]
                        t.enter(i, per)
                        cut()
                        if with_ada:
                            ada_products(la, 0)
                        cut()
                        if with_ada:
                            ada_products(la, 1)
                        hidden_low()
                        cut()
                        hidden()
                        if with_ada:
                            ada_store(la, c0 + i)
                    t.leave(count)

                if turns:
                    loop(turns, 1)
                if turns < NF - 1:
                    loop(NF - 1 - turns, 0)
                hidden_low()
                cut()

            def head_norm(src, groups, width, spread, sq):
                dve.wait_ge(s_sq, t.next(s_sq))
                chained(dve.tensor_reduce(st8[:, 2, 0:groups], sq, AX, ALU.add))
                dve.tensor_scalar(st8[:, 0, 0:groups], st8[:, 2, 0:groups], 1.0 / width, EPS,
                                  ALU.mult, ALU.add).then_inc(s_hvar, 1)
                dve.wait_ge(s_hsd, t.next(s_hsd))
                chained(dve.reciprocal(st8[:, 3, 0:groups], st8[:, 1, 0:groups]))
                chained(dve.tensor_tensor(spread, src, bc(st8[:, 3, 0:groups].unsqueeze(2), [P, groups, width]),
                                          ALU.mult))

            def low_out(dst, src, high):
                dve.wait_ge(s_xh, t.next(s_xh))
                dve.tensor_tensor(dst, src, high, ALU.subtract).then_inc(s_xl, 1)

            def exponents(n, e):
                if n < 8:
                    m = 1 << (n - 1)
                    b4, e4 = (a.rearrange("p (g two m) -> p g two m", two=2, m=m) for a in (b_, e))
                    shape = [P, 4 * S // (2 * m), m]
                    ref = bc(b4[:, :, 0, m - 1:m], shape)
                    if m < 64:
                        dve.tensor_tensor(e4[:, :, 1, :], b4[:, :, 1, :], ref, ALU.subtract)
                    else:
                        dve.tensor_copy(e4[:, :, 1, :], b4[:, :, 1, :])
                    dve.tensor_tensor(e4[:, :, 0, :], ref, b4[:, :, 0, :], ALU.subtract).then_inc(s_expo, 1)
                    return
                b4, e4 = (a.rearrange("p (h c m) -> p h c m", h=4, c=4) for a in (b_, e))
                chained(dve.tensor_tensor(e4[:, :, 0:2, :], bc(b4[:, :, 0:2, 63:64], [P, 4, 2, 64]), b4[:, :, 0:2, :],
                                          ALU.subtract))
                chained(dve.tensor_copy(e4[:, :, 2:4, :], b4[:, :, 2:4, :]))
                dve.tensor_tensor(e4[:, :, 0, :], e4[:, :, 0, :], bc(b4[:, :, 1, 63:64], [P, 4, 64]), ALU.add)
                dve.tensor_tensor(e4[:, :, 3, :], e4[:, :, 3, :], bc(b4[:, :, 2, 63:64], [P, 4, 64]),
                                  ALU.add).then_inc(s_expo, 1)

            def decayed(n, e):
                m = 1 << (n - 1)
                dve.wait_ge(s_decay, t.next(s_decay))
                e4, q4, k4 = (a.rearrange("p (g two m) -> p g two m", two=2, m=m) for a in (e, q_, k_))
                dve.tensor_tensor(e4[:, :, 1, :], e4[:, :, 1, :], q4[:, :, 1, :], ALU.mult)
                dve.tensor_tensor(e4[:, :, 0, :], e4[:, :, 0, :], k4[:, :, 0, :], ALU.mult).then_inc(s_z, 1)

            def select(n):
                dve.wait_ge(s_gram, t.next(s_gram))
                src = (PBf if n % 2 == 0 else TMf).rearrange("p (h s) -> p h s", s=P)
                if n == 0:
                    ins = dve.tensor_tensor(att, src, bc(ident.unsqueeze(1), [P, 8, P]), ALU.mult)
                elif n < 8:
                    mask = cst[:, C_LEVEL + (n - 1) * P:C_LEVEL + n * P].bitcast(I32)
                    ins = dve.copy_predicated(att, bc(mask.unsqueeze(1), [P, 8, P]), src)
                else:
                    ins = dve.tensor_copy(attX, src[:, 0:4, :])
                ins.then_inc(s_sel, 1)
                dve.wait_ge(s_sel, t.next(s_sel))

            def hgrn():
                norm(0, 1)
                cut()
                cut()
                for grp in range(2):
                    dve.wait_ge(s_key, t.next(s_key))
                    dve.tensor_scalar(b_, GUf, 0.0, None, ALU.min).then_inc(s_readD, 1)
                    if grp == 0:
                        cut()
                    dve.wait_ge(s_sigq, t.next(s_sigq))
                    dve.tensor_tensor(q_, E[1], PAf, ALU.mult).then_inc(s_readD, 1)
                    dve.wait_ge(s_readD, t.next(s_readD, 2))
                    if grp == 0:
                        cut()
                    dve.wait_ge(s_ln, t.next(s_ln))
                    chained(dve.tensor_tensor(E[1], b_, E[0], ALU.subtract))
                    chained(dve.tensor_tensor_scan(b_, cst[:, C_SCAN:C_SCAN + 4 * S], E[1], 0.0, ALU.mult, ALU.add))
                    if grp == 0:
                        cut()
                        cut()
                    for n in range(9):
                        if n < 8:
                            exponents(n + 1, E[(n + 1) % 3])
                        if n:
                            decayed(n, E[n % 3])
                            select(n - 1)
                        if grp == 0 and n < 8:
                            cut()
                    select(8)
                    by_head = lambda a: a.rearrange("p (g n) -> p g n", n=P)
                    head_norm(by_head(TMf), 8, P, by_head(q_), by_head(E[0]))
                    chained(dve.tensor_tensor(by_head(q_), by_head(q_), bc(vb[:, 0:P].unsqueeze(1), [P, 8, P]),
                                              ALU.mult))
                    by_tile = q_.rearrange("p (t n) -> p t n", t=NT)
                    dve.tensor_tensor(by_tile, by_tile, g_[:, :, grp * 512:(grp + 1) * 512], ALU.mult
                                      ).then_inc(s_on, 1)
                    d = slice(4 * grp, 4 * grp + 4)
                    low_out(xL[:, d, :].rearrange("p d s -> p (d s)"), PBf,
                            xH[:, d, :].rearrange("p d s -> p (d s)"))
                t.next(s_ot, 2)
                t.next(s_on, 2)
                t.next(s_readA, 4)
                for _ in range(4):
                    cut()

            def low_bank(b):
                dve.wait_ge(s_xh, t.next(s_xh))
                dve.tensor_tensor(xL2[:, b, :], PY[:, b, :], xH2[:, b, :], ALU.subtract).then_inc(s_xl, 1)

            def lambda_and_angles():
                prod = wrap[:, :, :, :].rearrange("p a t n -> p (a t n)")
                for n in range(2):
                    at = 3 * P + n * P
                    chained(dve.tensor_tensor(vb[:, at:at + 64], vb[:, at:at + 64], vb[:, at + 64:at + P], ALU.mult))
                    chained(dve.tensor_reduce(lam[:, n:n + 1], vb[:, at:at + 64], AX, ALU.add))
                chained(dve.tensor_scalar(vb[:, 2 * P:3 * P], vb[:, 2 * P:3 * P], 1.0 - LAMBDA_INIT, None, ALU.mult))
                chained(dve.tensor_copy(posf[:, :], posi[:, :]))
                raw_angle = ang[:, 0, :, :]
                chained(dve.tensor_tensor(raw_angle, bc(posf[:, :].unsqueeze(2), [P, NT, 8]),
                                          bc(cst[:, C_FREQ:C_FREQ + 8].unsqueeze(1), [P, NT, 8]), ALU.mult))
                chained(dve.tensor_scalar(turns_i[:, :, :], raw_angle, 1.0 / TWO_PI, None, ALU.mult))
                chained(dve.tensor_copy(turns_f[:, :, :], turns_i[:, :, :]))
                for part in (PI_A, PI_B, PI_C):
                    chained(dve.scalar_tensor_tensor(raw_angle, turns_f[:, :, :], -part, raw_angle,
                                                     ALU.mult, ALU.add))
                chained(dve.tensor_scalar(ang[:, 1, :, :], raw_angle, TWO_PI / 4, None, ALU.add))
                flat = ang[:, :, :, :].rearrange("p a t n -> p (a t n)")
                for op, edge, by in ((ALU.is_gt, TWO_PI / 2, -TWO_PI), (ALU.is_lt, -TWO_PI / 2, TWO_PI)):
                    chained(dve.tensor_scalar(prod, flat, edge, by, op, ALU.mult))
                    chained(dve.tensor_tensor(flat, flat, prod, ALU.add))
                dve.tensor_scalar(flat, flat, -3.1415925, 3.1415925, ALU.max, ALU.min).then_inc(s_trig, 1)
                dve.wait_ge(s_trigd, 1)
                chained(dve.tensor_tensor(lam[:, 4:5], lam[:, 3:4], lam[:, 2:3], ALU.subtract))
                chained(dve.tensor_scalar(lam[:, 5:6], lam[:, 4:5], LAMBDA_INIT, None, ALU.subtract))

            def mask_and_max(u, tile, banks):
                dve.wait_ge(s_score, t.next(s_score))
                src, dst, width = banks.rearrange("p (m s) -> p m s", s=S), p_[u % 2], P * (tile + 1)
                if tile:
                    dve.tensor_scalar(dst[:, :, 0:P], src[:, :, 0:P], 0.125, None, ALU.mult)
                dve.scalar_tensor_tensor(dst[:, :, tile * P:width], src[:, :, tile * P:width], 0.125,
                                         bc(causal.unsqueeze(1), [P, 4, P]), ALU.mult, ALU.add).then_inc(s_scored, 1)
                dve.wait_ge(s_scored, t.next(s_scored))
                chained(dve.tensor_reduce(stu[:, u % 2, 8:12], dst[:, :, 0:width], AX, ALU.max))
                dve.tensor_scalar(stu[:, u % 2, 0:4], stu[:, u % 2, 8:12], -1.0, None, ALU.mult).then_inc(s_max, 1)

            def difference(u, tile):
                width, stt = P * (tile + 1), stu[:, u % 2, :]
                dve.wait_ge(s_exp, t.next(s_exp))
                chained(dve.reciprocal(stt[:, 8:12], stt[:, 4:8]))
                chained(dve.tensor_scalar(stt[:, 12:14], stt[:, 10:12], lam[:, 5:6], None, ALU.mult))
                if u > 1:
                    dve.wait_ge(s_at, t.next(s_at))
                for h in range(2):
                    ins = dve.tensor_scalar(a_[u % 2][:, h, 0:width], p_[u % 2][:, h, 0:width], stt[:, 8 + h:9 + h],
                                            None, ALU.mult)
                chained(ins)
                for h in range(2):
                    ins = dve.scalar_tensor_tensor(a_[u % 2][:, h, 0:width], p_[u % 2][:, 2 + h, 0:width],
                                                   stt[:, 12 + h:13 + h], a_[u % 2][:, h, 0:width],
                                                   ALU.mult, ALU.add)
                ins.then_inc(s_a, 1)

            def rotate(x1, x2, cos, sin, y1, y2, tmp):
                dve.tensor_tensor(tmp[0], x1, cos, ALU.mult)
                dve.tensor_tensor(tmp[1], x2, sin, ALU.mult)
                dve.tensor_tensor(tmp[2], x2, cos, ALU.mult)
                chained(dve.tensor_tensor(tmp[3], x1, sin, ALU.mult))
                dve.tensor_tensor(y1, tmp[0], tmp[1], ALU.subtract)
                return dve.tensor_tensor(y2, tmp[2], tmp[3], ALU.add)

            def diff():
                lambda_and_angles()
                norm(1, 1)
                cut()
                cut()
                q16 = qk_.rearrange("p (g n) -> p g n", n=64)
                q4 = qk_.rearrange("p (t g n) -> p t g n", t=NT, n=64)
                shape = [P, NT, 8, 8]
                for c in range(4):
                    banks = GUf if c % 2 == 0 else PAf
                    if c:
                        dve.wait_ge(s_ot, t.next(s_ot))
                    head_norm(banks.rearrange("p (g n) -> p g n", n=64), 16, 64, q16,
                              sq_.rearrange("p (g n) -> p g n", n=64))
                    dve.sem_inc(s_readD, 1)
                    g = vb[:, P + (c // 2) * 64:P + (c // 2 + 1) * 64]
                    chained(dve.tensor_tensor(q16, q16, bc(g.unsqueeze(1), [P, 16, 64]), ALU.mult))
                    rotate(q4[:, :, :, 0:8], q4[:, :, :, 8:16], bc(ang[:, 1, :, :].unsqueeze(2), shape),
                           bc(ang[:, 0, :, :].unsqueeze(2), shape), q4[:, :, :, 0:8], q4[:, :, :, 8:16],
                           [rot[:, n] for n in range(4)]).then_inc(s_on, 1)
                    cut()
                    cut()
                t.next(s_ot)
                cut()
                cut()
                mask_and_max(0, 0, PBf)
                for u in range(8):
                    if u < 7:
                        mask_and_max(u + 1, (u + 1) // 4, PBf if u % 2 else PAf)
                    difference(u, u // 4)
                    if u == 4:
                        out_norm(0)
                out_norm(1)
                for b in range(4):
                    low_bank(b)
                t.next(s_at, 2)
                t.next(s_ot, 4)
                t.next(s_on, 6)
                t.next(s_readA, 2)
                cut()
                cut()

            def keys_rotated(src, branch):
                x4 = src.rearrange("p t (g n) -> p t g n", g=2)
                shape, d = [P, NT, 2, 32], kd_[:, branch]
                tmp = [rt_[:, n * P:(n + 1) * P].rearrange("p (t g n) -> p t g n", t=NT, g=2) for n in range(4)]
                chained(rotate(x4[:, :, :, 0:32], x4[:, :, :, 32:64], bc(cos2.unsqueeze(2), shape),
                               bc(sin2.unsqueeze(2), shape), d[:, :, :, 0, 0:32], d[:, :, :, 0, 32:64], tmp))
                return dve.tensor_copy(d[:, :, :, 1, :], d[:, :, :, 0, :])

            def gated(u, tile):
                width, stt = P * (tile + 1), stu[:, u % 2, :]
                g, b = u // 2 % 2, u % 2
                dve.wait_ge(s_exp, t.next(s_exp))
                chained(dve.reciprocal(stt[:, 8:12], stt[:, 4:8]))
                gate = gates[:, tile, 2 * g:2 * g + 2, :, 1 + b].rearrange("p h c -> p c h")
                pairs = lambda a: a.rearrange("p (c h) -> p c h", c=2)
                chained(dve.tensor_tensor(pairs(stt[:, 12:16]), pairs(stt[:, 8:12]), gate, ALU.mult))
                if u > 1:
                    dve.wait_ge(s_at, t.next(s_at))
                for m in range(4):
                    ins = dve.tensor_scalar(a2_[u % 2][:, m, 0:width], p_[u % 2][:, m, 0:width],
                                            stt[:, 12 + m:13 + m], None, ALU.mult)
                ins.then_inc(s_a, 1)

            def nsa(l):
                norm(l, 1)
                cut()
                cut()
                dve.wait_ge(s_eaten, t.next("done", 2))
                for i in range(NT):
                    dve.tensor_copy(cd_[:, i], bc(GU[:, i, 0:256].rearrange("p (m n) -> p m n", n=64).unsqueeze(2),
                                                  [P, 4, 2, 64]))
                dve.tensor_copy(v2_[:, 0], GU[:, :, 384:512])
                keys_rotated(GU[:, :, 256:384], 0).then_inc(s_on, 1)
                dve.wait_ge(s_on, t.next(s_on))
                dve.sem_inc(s_readD, 1)
                cut(4 * 280)
                cut(4 * 280)
                dve.wait_ge(s_eaten, t.next("done", 2))
                for i in range(NT):
                    x3 = PY[:, i, :].rearrange("p (h n) -> p h n", n=64)
                    y3 = qr_[:, i, :].rearrange("p (h n) -> p h n", n=64)
                    tmp = [rt_[:, n * S:(n + 1) * S].rearrange("p (h n) -> p h n", n=32) for n in range(4)]
                    ins = rotate(x3[:, :, 0:32], x3[:, :, 32:64], bc(cos2[:, i:i + 1, :], [P, 8, 32]),
                                 bc(sin2[:, i:i + 1, :], [P, 8, 32]), y3[:, :, 0:32], y3[:, :, 32:64], tmp)
                    if i == 0:
                        chained(ins)
                ins.then_inc(s_on, 1)
                dve.wait_ge(s_on, t.next(s_on))
                dve.sem_inc(s_readD, 1)
                cut()
                cut()
                dve.wait_ge(s_gate, t.next(s_gate))
                t.next("done", 2)
                dve.tensor_copy(v2_[:, 1], GU[:, :, 128:256])
                keys_rotated(GU[:, :, 0:128], 1).then_inc(s_on, 1)
                dve.wait_ge(s_on, t.next(s_on))
                dve.sem_inc(s_readD, 1)
                cut()
                cut()
                dve.wait_ge(s_cmp, t.next(s_cmp, 2))
                kv = PY[0:NCMP, 3, 0:256].rearrange("p (m n) -> p m n", n=64)
                dve.tensor_copy(vc_[0:NCMP], kv[:, 2:4, :])
                shape = [NCMP, 2, 32]
                chained(rotate(kv[:, 0:2, 0:32], kv[:, 0:2, 32:64],
                               bc(cst[0:NCMP, C_CCOS:C_CCOS + 32].unsqueeze(1), shape),
                               bc(cst[0:NCMP, C_CSIN:C_CSIN + 32].unsqueeze(1), shape),
                               kcd[0:NCMP, :, 0, 0:32], kcd[0:NCMP, :, 0, 32:64], [kct[0:NCMP, n] for n in range(4)]))
                dve.tensor_copy(kcd[0:NCMP, :, 1, :], kcd[0:NCMP, :, 0, :]).then_inc(s_kc, 1)
                dve.wait_ge(s_gm, 48 * (l - 1))
                dve.tensor_tensor(ws_, ws_, bc(cst[:, C_TRIL:C_TRIL + P].unsqueeze(1), [P, 8, P]),
                                  ALU.mult).then_inc(s_wm, 1)
                dve.wait_ge(s_readA, t.next(s_readA))
                for i in range(NT):
                    chained(dve.bn_stats(bn_[:, i, :], vg_[:, i, :]))
                for i in range(NT):
                    chained(dve.bn_aggr(mv_[:, i, :], bn_[:, i, :]))
                dve.tensor_scalar(mv_[:, :, 1], mv_[:, :, 1], EPS, None, ALU.add).then_inc(s_bnv, 1)
                cut()
                cut()
                dve.wait_ge(s_bns, t.next(s_bns))
                chained(dve.reciprocal(mv_[:, :, 1], mv_[:, :, 1]))
                for i in range(NT):
                    ins = dve.tensor_scalar(vg_[:, i, :], vg_[:, i, :], mv_[:, i, 0:1], mv_[:, i, 1:2],
                                            ALU.subtract, ALU.mult)
                chained(ins)
                chained(dve.tensor_tensor(vg_, vg_, bc(ln_[:, 0:1, :], [P, NT, 512]), ALU.mult))
                dve.tensor_tensor(vg_, vg_, bc(ln_[:, 1:2, :], [P, NT, 512]), ALU.add).then_inc(s_vn, 1)
                dve.wait_ge(s_cmp, t.next(s_cmp))
                dve.tensor_copy(kcT[:, :, 0:NCMP], PY[:, 2, 0:32].rearrange("p (g n) -> p g n", g=2)[:, :, 0:NCMP]
                                ).then_inc(s_kc, 1)
                cut()
                cut()
                cut()
                cut()
                dve.wait_ge(s_sv, t.next(s_sv))
                y4, u4, p4 = (a.rearrange("p t (g n) -> p t g n", n=64) for a in (y_, u_, PY[:, 2:4, :]))
                at = 2 * ND + 12 * ND + (l - 2) * 8
                chained(dve.tensor_tensor(y4, p4, bc(cols[:, at:at + 8].unsqueeze(1).unsqueeze(3), [P, NT, 8, 64]),
                                          ALU.add))
                dve.tensor_tensor(y4, y4, u4, ALU.mult).then_inc(s_yb, 1)
                cut()
                cut()
                cut()
                cut()
                low_out(xL[:, 4:8, :].rearrange("p d s -> p (d s)"), PBf, xH[:, 4:8, :].rearrange("p d s -> p (d s)"))
                dve.wait_ge(s_cmp, t.next(s_cmp))
                for c in range(2):
                    for i in range(NT):
                        ins = dve.tensor_scalar(pc_[:, c, 4 * i:4 * i + 4, :],
                                                TM[:, c, 64 * i:64 * i + 64].rearrange("p (m n) -> p m n", n=16
                                                                                       )[:, :, 0:NCMP],
                                                0.125, None, ALU.mult)
                chained(ins)
                masked = lambda at, i: bc(cst[:, at + i * NCMP:at + (i + 1) * NCMP].unsqueeze(1), [P, 4, NCMP])
                for c in range(2):
                    for i in range(NT):
                        ins = dve.tensor_tensor(pc_[:, c, 4 * i:4 * i + 4, :], pc_[:, c, 4 * i:4 * i + 4, :],
                                                masked(C_CMPN, i), ALU.add)
                chained(ins)
                spread = lambda k: bc(st8[:, k, 0:16].unsqueeze(2), [P, 16, NCMP])
                chained(dve.tensor_reduce(st8[:, 0, 0:16], pcf, AX, ALU.max))
                dve.tensor_tensor(pcf, pcf, spread(0), ALU.subtract).then_inc(s_cx, 1)
                dve.wait_ge(s_ce, t.next(s_ce))
                chained(dve.tensor_reduce(st8[:, 1, 0:16], pcf, AX, ALU.add))
                chained(dve.reciprocal(st8[:, 2, 0:16], st8[:, 1, 0:16]))
                for c in range(2):
                    view = lambda k: st8[:, k, 8 * c:8 * c + 8].rearrange("p (t h) -> p t h", t=NT)
                    ins = dve.tensor_tensor(view(3), view(2), gates[:, :, :, c, 0], ALU.mult)
                chained(ins)
                chained(dve.tensor_tensor(pcf, pcf, spread(3), ALU.mult))
                for c in range(2):
                    for i in range(NT):
                        ins = dve.tensor_tensor(pc_[:, c, 4 * i:4 * i + 4, :], pc_[:, c, 4 * i:4 * i + 4, :],
                                                masked(C_CMPM, i), ALU.mult)
                ins.then_inc(s_pc, 1)
                mask_and_max(0, 0, PBf)
                for u in range(8):
                    if u < 7:
                        mask_and_max(u + 1, (u + 1) // 4, PBf if u % 2 else PAf)
                    gated(u, u // 4)
                t.next(s_at, 2)
                low_out(xL[:, 0:4, :].rearrange("p d s -> p (d s)"), PBf, xH[:, 0:4, :].rearrange("p d s -> p (d s)"))
                cut()
                cut()
                for h in range(2):
                    cols_h = slice(h * 512, (h + 1) * 512)
                    dve.wait_ge(s_eaten, t.next("done", 14 if h == 0 else 2))
                    dve.tensor_tensor(xn[:, :, cols_h], GU[:, :, :], sg_[0][:, :, cols_h], ALU.mult)
                    chained(dve.tensor_tensor(y_, PY[:, 0:2, :], sg_[1][:, :, cols_h], ALU.mult))
                    dve.tensor_tensor(xn[:, :, cols_h], xn[:, :, cols_h], y_, ALU.add).then_inc(s_merged, 1)
                    dve.wait_ge(s_merged, t.next(s_merged))
                    if h == 0:
                        cut()
                        cut()
                for b in range(4):
                    low_bank(b)
                cut()
                cut()
                t.next(s_readA, 7)

            def out_norm(tile):
                by_head = lambda a: a.rearrange("p (g n) -> p g n", n=P)
                head_norm(by_head(GUf), 8, P, by_head(on_[tile]), by_head(xn[:, 0, :]))
                dve.sem_inc(s_readD, 1)
                dve.tensor_tensor(by_head(on_[tile]), by_head(on_[tile]), bc(vb[:, 2 * P:3 * P].unsqueeze(1),
                                  [P, 8, P]), ALU.mult).then_inc(s_on, 1)

            dve.memset(ones[:, :], 1.0).then_inc(s_ones, 1)
            dve.sem_inc(s_split, RING)
            dve.sem_inc(s_adafree, ADA_RING)
            dve.wait_ge(s_cs, 1)
            chained(dve.tensor_copy(cols[:, :], TM[:, 0, 0:P]))
            chained(dve.tensor_copy(peT[:, :], TM[:, 0, P:P + 64]))
            dve.wait_ge(s_col, 2)
            chained(dve.tensor_copy(bT[:, :], TM[:, 1, 0:4 * MODS]))
            for c in range(ADA_FIRST):
                ada_products(0, 0)
                ada_products(0, 1)
                ada_store(0, c)
            cut()
            cut()
            for n, (l, j) in enumerate(PHASES):
                if j != 1:
                    ffn(l, j)
                elif l == 0:
                    hgrn()
                elif l == 1:
                    diff()
                else:
                    nsa(l)
                if n + 1 < len(PHASES):
                    cut()
                    cut()
                residual(3 * NF if j != 1 else PIECES[l] - (22 if l > 1 else 0))
            if len(PHASES) == 12:
                tile_roots()
                dve.wait_ge(s_const, 16 * (N_CONST + 1))
                fg = ln_.rearrange("p a n -> p (a n)")
                for i in range(NT):
                    ins = dve.scalar_tensor_tensor(x[:, i, :], x[:, i, :], st[:, 6 + i:7 + i], fg, ALU.mult, ALU.mult)
                    if i == 0:
                        chained(ins)
                ins.then_inc(s_x, 1)

        @block.tensor
        def _(pe):
            t = Tally(s_split=RING)

            def times_three(outs, aH, aL, wh, wl, first, last):
                n = len(outs)
                for i in range(n):
                    pe.matmul(outs[i], aH, wh[i], start=first, stop=False)
                for i in range(n):
                    pe.matmul(outs[i], aH, wl[i], start=False, stop=False)
                for i in range(n):
                    ins = pe.matmul(outs[i], aL, wh[i], start=False, stop=last)
                return ins

            def gate_broadcast():
                pe.wait_ge(s_gcol, t.next(s_gcol))
                for d in range(ND):
                    ins = pe.matmul(TM[:, d // 4, (d % 4) * P:(d % 4 + 1) * P], shf[:, d * P:(d + 1) * P], ident,
                                    start=True, stop=True)
                ins.then_inc(s_gp, 1)

            def norm(l, j):
                gate_broadcast()
                pe.wait_ge(s_xn, t.next(s_xn, NT))
                for d in range(ND):
                    for i in range(NT):
                        ins = pe.transpose(PYt[:, d, i * P:(i + 1) * P], xn[:, i, d * P:(d + 1) * P], ident)
                    if d % 2:
                        ins.then_inc(s_xt, 1)

            def up(q, fresh=False):
                slot = t.next("piece") % RING
                pe.wait_ge(s_split, t.next(s_split))
                for i in range(NT):
                    for k in range(4):
                        if fresh and i == 0 and k % 2 == 0:
                            pe.wait_ge(s_xl, t.next(s_xl))
                        d = 4 * q + k
                        a, b = slice(i * P, (i + 1) * P), slice(k * 512, (k + 1) * 512)
                        ins = times_three([GU[:, i, :]], xH[:, d, a], xL[:, d, a], [wH[:, slot, b]], [wL[:, slot, b]],
                                          d == 0, d == ND - 1)
                ins.then_inc(s_eaten, 1)

            def turn_hidden():
                for i in range(NT):
                    for f in range(2):
                        ins = pe.transpose(TM[:, 0, f * S + i * P:f * S + (i + 1) * P],
                                           sh[:, 1, i, f * P:(f + 1) * P], ident)
                ins.then_inc(s_ht, 1)

            def down(first, last):
                slot = t.next("piece") % RING
                pe.wait_ge(s_split, t.next(s_split))
                pe.wait_ge(s_hl, t.next(s_hl))
                for i in range(NT):
                    for f in range(2):
                        a = slice(i * P, (i + 1) * P)
                        halves = [slice(f * D + h * 512, f * D + (h + 1) * 512) for h in range(2)]
                        ins = times_three([PY[:, 2 * i + h, :] for h in range(2)], hH[:, f, a], hL[:, f, a],
                                          [wH[:, slot, b] for b in halves], [wL[:, slot, b] for b in halves],
                                          first and f == 0, last and f == 1)
                ins.then_inc(s_eaten, 1)

            def ada_sums():
                pe.wait_ge(s_acc, t.next(s_acc))
                for k in range(4):
                    ins = pe.matmul(TM[:, 1, k:k + 1], acc[:, k * P:(k + 1) * P], ones[:, :], start=True, stop=True)
                ins.then_inc(s_modp, 1)

            def ffn(l, j):
                norm(l, j)
                up(0, True)
                up(1, True)
                pe.wait_ge(s_gb, t.next(s_gb))

                def turn(with_ada, first=False):
                    pe.wait_ge(s_h, t.next(s_h))
                    up(0)
                    turn_hidden()
                    up(1)
                    if with_ada:
                        ada_sums()
                    down(first, False)

                def loop(count, with_ada):
                    with pe.Fori(0, count) as i:
                        t.enter(i, [("piece", 3), (s_split, 3), (s_h, 1), (s_hl, 1), (s_acc, int(with_ada))])
                        turn(with_ada)
                    t.leave(count)

                turns = ada_turns(l, j)[2]
                turn(turns > 0, True)
                if turns:
                    loop(turns - 1, True)
                rest = NF - 1 - max(turns, 1)
                if rest:
                    loop(rest, False)
                pe.wait_ge(s_h, t.next(s_h))
                turn_hidden()
                down(False, True)

            def by_token(banks, q, fresh=False, width=512, tiles=(0, ND - 1)):
                slot = t.next("piece") % RING
                pe.wait_ge(s_split, t.next(s_split))
                for i in range(NT):
                    for k in range(4):
                        if fresh and i == 0 and k % 2 == 0:
                            pe.wait_ge(s_xl, t.next(s_xl))
                        d = 4 * q + k
                        a, b = slice(i * P, (i + 1) * P), slice(k * width, (k + 1) * width)
                        ins = times_three([banks[i]], xH[:, d, a], xL[:, d, a], [wH[:, slot, b]], [wL[:, slot, b]],
                                          d == tiles[0], d == tiles[1])
                ins.then_inc(s_eaten, 1)

            def by_channel(banks, q, fresh=False):
                slot = t.next("piece") % RING
                pe.wait_ge(s_split, t.next(s_split))
                for k in range(4):
                    if fresh and k % 2 == 0:
                        pe.wait_ge(s_xl, t.next(s_xl))
                    d = 4 * q + k
                    for n in range(4):
                        w = slice(k * 512 + n * P, k * 512 + (n + 1) * P)
                        o = banks[:, n * S:(n + 1) * S]
                        pe.matmul(o, wH[:, slot, w], xH[:, d, :], start=(d == 0 and n % 2 == 0), stop=False,
                                  skip_group_check=True)
                        pe.matmul(o, wH[:, slot, w], xL[:, d, :], start=False, stop=False, skip_group_check=True)
                        ins = pe.matmul(o, wL[:, slot, w], xH[:, d, :], start=False, stop=(d == ND - 1),
                                        skip_group_check=True)
                ins.then_inc(s_eaten, 1)

            def project(q, h, fresh=False):
                by_token([PY[:, 2 * i + h, :] for i in range(NT)], q, fresh)

            def hgrn():
                norm(0, 1)
                pe.wait_ge(s_gb, t.next(s_gb))
                A, B = [GU[:, i, :] for i in range(NT)], [PY[:, i, :] for i in range(NT)]
                by_channel(GUf, 0, True)
                by_channel(GUf, 1, True)
                by_channel(PAf, 0)
                by_channel(PAf, 1)
                for banks in (A, B):
                    pe.wait_ge(s_readD, t.next(s_readD))
                    by_token(banks, 0)
                    by_token(banks, 1)
                for grp in range(2):
                    if grp == 1:
                        pe.wait_ge(s_readD, t.next(s_readD, 2))
                    for n in range(9):
                        if n:
                            pe.wait_ge(s_z, t.next(s_z))
                        if n > 1:
                            pe.wait_ge(s_sel, t.next(s_sel))
                        dst = (PBf if n % 2 == 0 else TMf).rearrange("p (h s) -> p h s", s=P)
                        e = E[n % 3].rearrange("p (h s) -> p h s", s=P)
                        kk, qq = (k_.rearrange("p (h s) -> p h s", s=P), q_.rearrange("p (h s) -> p h s", s=P)
                                  ) if n == 0 else (e, e)
                        for h in range(8 if n < 8 else 4):
                            if n < 8:
                                ins = pe.matmul(dst[:, h, :], kk[:, h, :], qq[:, h, :], start=True, stop=True)
                            else:
                                ins = pe.matmul(dst[:, h, :], kk[:, 2 * h, :], qq[:, 2 * h + 1, :],
                                                start=True, stop=True)
                        ins.then_inc(s_gram, 1)
                        if grp == 0 and n < 8:
                            if n == 0 or n == 2:
                                pe.wait_ge(s_readA, t.next(s_readA))
                            if n == 4 or n == 6:
                                pe.wait_ge(s_readA, t.next(s_readA))
                            if n < 4:
                                by_token(A if n < 2 else B, n % 2)
                            else:
                                by_channel(GUf if n < 6 else PAf, n % 2)
                    pe.wait_ge(s_sel, t.next(s_sel, 2))
                    for h in range(4):
                        c = slice((4 * grp + h) * P, (4 * grp + h + 1) * P)
                        pe.matmul(TM[:, 0, h * P:(h + 1) * P], att[:, 2 * h, :], v_[:, 0, c], start=True, stop=True)
                        pe.matmul(TM[:, 1, h * P:(h + 1) * P], att[:, 2 * h + 1, :], v_[:, 1, c],
                                  start=True, stop=False)
                        ins = pe.matmul(TM[:, 1, h * P:(h + 1) * P], attX[:, h, :], v_[:, 0, c],
                                        start=False, stop=True)
                    ins.then_inc(s_o, 1)
                    pe.wait_ge(s_on, t.next(s_on))
                    for h in range(4):
                        for i in range(NT):
                            ins = pe.transpose(PBf[:, h * S + i * P:h * S + (i + 1) * P],
                                               q_[:, i * 512 + h * P:i * 512 + (h + 1) * P], ident)
                    ins.then_inc(s_ot, 1)
                pe.wait_ge(s_xl, t.next(s_xl, 2))
                for h in range(2):
                    for q in range(2):
                        project(q, h)

            def scores(u, tile, keys, heads, queries=qT):
                banks = (PBf if u % 2 == 0 else PAf).rearrange("p (m s) -> p m s", s=S)
                if u > 1:
                    pe.wait_ge(s_scored, t.next(s_scored))
                for n, h in enumerate(heads):
                    for c in range(2):
                        r = slice(c * 64, (c + 1) * 64)
                        ins = pe.matmul(banks[:, 2 * c + n, 0:P * (tile + 1)], queries[r, h, tile * P:(tile + 1) * P],
                                        keys(h)[r, 0:P * (tile + 1)], start=True, stop=True)
                ins.then_inc(s_score, 1)

            def turn_weights(u, tile, maps):
                pe.wait_ge(s_a, t.next(s_a))
                for h in range(2):
                    for k in range(tile + 1):
                        n = h * (tile + 1) + k
                        ins = pe.transpose(TM[:, u % 2, n * P:(n + 1) * P], a_[u % 2][:, h, k * P:(k + 1) * P], ident)
                ins.then_inc(s_at, 1)

            def diff():
                norm(1, 1)
                pe.wait_ge(s_gb, t.next(s_gb))
                A, B = [GU[:, i, :] for i in range(NT)], [PY[:, i, :] for i in range(NT)]
                for c in range(6):
                    if c > 1:
                        pe.wait_ge(s_readD, t.next(s_readD))
                    for q in range(2):
                        by_token(B if c % 2 else A, q, c == 0)
                    if c:
                        turn_chunk(c - 1)
                pe.wait_ge(s_readA, t.next(s_readA, 2))
                pe.wait_ge(s_aT, t.next(s_aT))
                keys = lambda h: kT[:, h, :]
                heads = lambda u: (2 * (u % 4), 2 * (u % 4) + 1)
                scores(0, 0, keys, heads(0))
                scores(1, 0, keys, heads(1))
                for u in range(8):
                    tile = u // 4
                    turn_weights(u, tile, 2)
                    if u < 6:
                        scores(u + 2, (u + 2) // 4, keys, heads(u + 2))
                    if u == 4:
                        pe.wait_ge(s_readD, t.next(s_readD))
                    pe.wait_ge(s_aT, t.next(s_aT))
                    for n, h in enumerate(heads(u)):
                        for k in range(tile + 1):
                            m = n * (tile + 1) + k
                            ins = pe.matmul(GUf[:, h * P:(h + 1) * P], aT[u % 2][:, m * P:(m + 1) * P],
                                            vB[:, k, h * P:(h + 1) * P], start=(k == 0), stop=(k == tile))
                    if u % 4 == 3:
                        ins.then_inc(s_o, 1)
                t.next(s_scored, 2)
                pe.wait_ge(s_readD, t.next(s_readD))
                pe.wait_ge(s_on, t.next(s_on, 2))
                for d in range(ND):
                    for i in range(NT):
                        ins = pe.transpose(PYt[:, d, i * P:(i + 1) * P], on_[i][:, d * P:(d + 1) * P], ident)
                    if d % 2:
                        ins.then_inc(s_ot, 1)
                pe.wait_ge(s_xl, t.next(s_xl, 4))
                for h in range(2):
                    for q in range(2):
                        project(q, h)

            def turn_chunk(c):
                if c > 3:
                    return
                pe.wait_ge(s_on, t.next(s_on))
                if c:
                    pe.wait_ge(s_aT, t.next(s_aT))
                for h in range(4):
                    for i in range(NT):
                        ins = pe.transpose(TMf[:, h * S + i * P:h * S + (i + 1) * P],
                                           qk_[:, i * 512 + h * P:i * 512 + (h + 1) * P], ident)
                ins.then_inc(s_ot, 1)

            def turn_tiles(dst, src):
                for d in range(4):
                    for i in range(NT):
                        ins = pe.transpose(dst[:, d * S + i * P:d * S + (i + 1) * P], src(i, d), ident)
                ins.then_inc(s_ot, 1)

            def nsa(l):
                norm(l, 1)
                A, B = [GU[:, i, :] for i in range(NT)], [PY[:, i, :] for i in range(NT)]

                def chunk(banks, fresh=False, width=512):
                    for q in range(2):
                        by_token([b[:, 0:width] for b in banks], q, fresh, width)

                chunk(A, True)
                pe.wait_ge(s_gb, t.next(s_gb))
                chunk(B)
                pe.wait_ge(s_on, t.next(s_on))
                turn_tiles(TMf, lambda i, m: cd_[:, i, m].rearrange("p c n -> p (c n)"))
                pe.wait_ge(s_readD, t.next(s_readD))
                chunk(A, width=280)
                pe.wait_ge(s_on, t.next(s_on))
                pe.wait_ge(s_aT, t.next(s_aT))
                turn_tiles(TMf, lambda i, h: qr_[:, i, h * P:(h + 1) * P])
                pe.wait_ge(s_w1, 80 * (l - 1))
                for j in range(2):
                    for n in range(16):
                        w = w1_[j][:, n * P:(n + 1) * P]
                        pe.matmul(PY[:, 2, 64 * j:64 * j + 30], w, cT_[:, j, :, 2 * n:2 * n + 16 * (NCMP - 1) + 1:16],
                                  start=(n == 0), stop=(n == 15))
                    for n in range(16):
                        w = w1_[j][:, n * P:(n + 1) * P]
                        at = (l - 2) * 32 + j * 16 + n
                        ins = pe.matmul(PY[:, 2, 64 * j + 32:64 * j + 33], w, peT[:, at:at + 1],
                                        start=(n == 0), stop=(n == 15))
                ins.then_inc(s_cmp, 1)
                pe.wait_ge(s_readD, t.next(s_readD))
                chunk(B)
                pe.wait_ge(s_hc, t.next(s_hc))
                for j in range(2):
                    for g in range(2):
                        m = 2 * j + g
                        ins = pe.matmul(PY[0:NCMP, 3, m * 64:(m + 1) * 64], hc_[:, j, g * NCMP:(g + 1) * NCMP],
                                        w2_[:, j, :], start=True, stop=True)
                ins.then_inc(s_cmp, 1)
                pe.wait_ge(s_on, t.next(s_on))
                pe.wait_ge(s_aT, t.next(s_aT))
                turn_tiles(TMf, lambda i, m: kd_[:, m // 2, i, m % 2].rearrange("p c n -> p (c n)"))
                pe.wait_ge(s_readD, t.next(s_readD))
                chunk(A)
                pe.wait_ge(s_kc, t.next(s_kc))
                for g in range(2):
                    ins = pe.transpose(PY[:, 2, g * 16:g * 16 + NCMP],
                                       kcd[0:NCMP, g].rearrange("p c n -> p (c n)"), ident[0:NCMP, 0:NCMP])
                ins.then_inc(s_cmp, 1)
                pe.wait_ge(s_wm, t.next(s_wm))
                pe.wait_ge(s_aT, t.next(s_aT))
                for g in range(8):
                    ins = pe.transpose(TMf[:, g * P:(g + 1) * P], ws_[:, g, :], ident)
                ins.then_inc(s_ot, 1)
                pe.wait_ge(s_readA, t.next(s_readA))
                chunk(B)
                pe.wait_ge(s_vn, t.next(s_vn))
                pe.wait_ge(s_kc, t.next(s_kc))
                pe.wait_ge(s_aT, t.next(s_aT))
                for g in range(8):
                    for i in range(NT):
                        ins = pe.matmul(PY[:, 2 + i, g * 64:(g + 1) * 64], wsT[:, g * P:(g + 1) * P],
                                        vg_[:, i, g * 64:(g + 1) * 64], start=True, stop=True)
                ins.then_inc(s_sv, 1)
                pe.wait_ge(s_readA, t.next(s_readA))
                chunk(A)
                pe.wait_ge(s_readA, t.next(s_readA))
                chunk(B)
                pe.wait_ge(s_readA, t.next(s_readA))
                chunk(A)
                pe.wait_ge(s_yb, t.next(s_yb))
                turn_tiles(PBf, lambda i, d: y_[:, i, d * P:(d + 1) * P])
                for i in range(NT):
                    for h in range(4):
                        for c in range(2):
                            r = slice(c * 64, (c + 1) * 64)
                            at = 64 * i + 16 * h
                            ins = pe.matmul(TM[:, c, at:at + NCMP], qT2[r, h, i * P:(i + 1) * P],
                                            kcT[r, h // 2, 0:NCMP], start=True, stop=True)
                ins.then_inc(s_cmp, 1)
                keys = lambda u: (lambda h: kT2[:, u % 2, u // 2 % 2, :])
                pairs = lambda u: (u // 2 % 2 * 2, u // 2 % 2 * 2 + 1)
                pe.wait_ge(s_xl, t.next(s_xl))
                scores(0, 0, keys(0), pairs(0), qT2)
                pe.wait_ge(s_readA, t.next(s_readA))
                scores(1, 0, keys(1), pairs(1), qT2)
                pe.wait_ge(s_pc, t.next(s_pc))
                for i in range(NT):
                    if i:
                        pe.wait_ge(s_aT, t.next(s_aT))
                    for h in range(8):
                        ins = pe.transpose(TMf[0:NCMP, h * P:(h + 1) * P], pc_[:, h % 2, 4 * i + h // 2, :], ident)
                    ins.then_inc(s_ot, 1)
                pe.wait_ge(s_readA, t.next(s_readA))
                pe.wait_ge(s_aT, t.next(s_aT))
                for i in range(NT):
                    for h in range(8):
                        pe.matmul(GU[:, i, h * 64:(h + 1) * 64], xn[0:NCMP, i, h * P:(h + 1) * P],
                                  vc_[0:NCMP, h // 4, :], start=(h == 0), stop=False, skip_group_check=True)
                for u in range(8):
                    tile, g, b = u // 4, u // 2 % 2, u % 2
                    pe.wait_ge(s_a, t.next(s_a))
                    for m in range(4):
                        for k in range(tile + 1):
                            dst = TMf[:, (2 * m + k) * P:(2 * m + k + 1) * P] if tile else \
                                TM[:, u % 2, m * P:(m + 1) * P]
                            ins = pe.transpose(dst, a2_[u % 2][:, m, k * P:(k + 1) * P], ident)
                    ins.then_inc(s_at, 1)
                    if u < 6:
                        scores(u + 2, (u + 2) // 4, keys(u + 2), pairs(u + 2), qT2)
                    pe.wait_ge(s_aT, t.next(s_aT))
                    for m in range(4):
                        h = 2 * (2 * g + m % 2) + m // 2
                        for k in range(tile + 1):
                            n = m * (tile + 1) + k
                            ins = pe.matmul(GU[:, tile, h * 64:(h + 1) * 64], aT2[u % 2][:, n * P:(n + 1) * P],
                                            v2_[:, b, k, g * 64:(g + 1) * 64], start=False,
                                            stop=(b == 1 and k == tile), skip_group_check=True)
                    if u % 4 == 3:
                        ins.then_inc(s_o, 1)
                pe.wait_ge(s_scored, t.next(s_scored, 2))
                pe.wait_ge(s_readA, t.next(s_readA, 2))
                turn_tiles(PBf, lambda i, d: yo_[:, i, d * P:(d + 1) * P])
                pe.wait_ge(s_xl, t.next(s_xl))
                for h in range(2):
                    if h:
                        pe.wait_ge(s_merged, t.next(s_merged))
                    by_token(A, 0, tiles=(0, 3))
                    by_token(B, 1, tiles=(4, 7))
                pe.wait_ge(s_merged, t.next(s_merged))
                for d in range(ND):
                    for i in range(NT):
                        ins = pe.transpose(PYt[:, d, i * P:(i + 1) * P], xn[:, i, d * P:(d + 1) * P], ident)
                    if d % 2:
                        ins.then_inc(s_ot, 1)
                pe.wait_ge(s_xl, t.next(s_xl, 4))
                for h in range(2):
                    for q in range(2):
                        project(q, h)

            pe.sem_inc(s_eaten, RING)
            pe.wait_ge(s_ones, 1)
            pe.wait_ge(s_const, N_CONST * 16)
            pe.transpose(TM[:, 0, 0:P], rows[:, 0, :], ident)
            pe.transpose(TM[:, 0, P:P + 64], rows[0:64, 5, :], ident[0:64, 0:64]).then_inc(s_col, 1)
            for l in range(4):
                ins = pe.transpose(TM[:, 1, l * MODS:(l + 1) * MODS], rows[0:MODS, 1 + l, :], ident[0:MODS, 0:MODS])
            ins.then_inc(s_col, 1)
            for c in range(ADA_FIRST):
                ada_sums()
            for l, j in PHASES:
                if j != 1:
                    ffn(l, j)
                elif l == 0:
                    hgrn()
                elif l == 1:
                    diff()
                else:
                    nsa(l)


def table():
    import numpy as np
    a = np.zeros((P, C_END), np.float32)
    p = np.arange(P)
    a[:, C_ID:C_ID + P] = np.eye(P)
    a[:, C_CAUSAL:C_CAUSAL + P] = np.where(p[None, :] <= p[:, None], 0.0, NEG)
    a[:, C_TRIL:C_TRIL + P] = p[None, :] <= p[:, None]
    a[:, C_SCAN:C_SCAN + 4 * S] = np.arange(4 * S) % 64 != 0
    for n in range(NLEVEL):
        m = 1 << n
        a[:, C_LEVEL + n * P:C_LEVEL + (n + 1) * P] = ((p[:, None] // (2 * m) == p[None, :] // (2 * m))
                                                       & (p[:, None] // m % 2 == 0) & (p[None, :] // m % 2 == 1))
    ends = np.arange(NCMP) * 16 + 31
    token = np.arange(S)
    seen = (ends[None, :] <= token[:, None]).reshape(NT, P, NCMP).transpose(1, 0, 2).reshape(P, -1)
    a[:, C_CMPM:C_CMPM + NT * NCMP] = seen
    a[:, C_CMPN:C_CMPN + NT * NCMP] = np.where(seen, 0.0, NEG)
    inv = np.float32(1.0) / (10000.0 ** (np.arange(0, 64, 2) / 64)).astype(np.float32)
    for at, f in ((C_COS, np.cos), (C_SIN, np.sin)):
        v = f((token.astype(np.float32)[:, None] * inv[None, :]).astype(np.float64))
        a[:, at:at + NT * 32] = v.reshape(NT, P, 32).transpose(1, 0, 2).reshape(P, -1)
    for at, f in ((C_CCOS, np.cos), (C_CSIN, np.sin)):
        a[0:NCMP, at:at + 32] = f((ends.astype(np.float32)[:, None] * inv[None, :]).astype(np.float64))
    a[:, C_FREQ:C_FREQ + 8] = 500000.0 ** (-np.arange(0, 16, 2) / 16)
    return a


_INS = ["x", "positions", "ada_w", "ada_b", "ffn_wi", "ffn_wo", "a_w_in", "a_w_out", "a_onorm", "b_w_in", "b_w_out",
        "b_qk_g", "b_lam", "b_subln", "ada_w_2", "ada_b_2", "ffn_w_in_2", "ffn_w_out_2", "mix_w_in_2",
        "cmp_pe_2", "cmp_w1_2", "cmp_w2_2", "gm_ln_g_2", "gm_ln_b_2", "gm_ws_2", "proj_a_2", "proj_b_2", "w_out_2",
        "final_g_2"]


def kernel(**inputs):
    import numpy as _np
    import concourse.bacc as _bacc
    from concourse.bass_utils import run_bass_kernel_spmd as _run

    nc = _bacc.Bacc("TRN2", target_bir_lowering=False, num_devices=1)
    arrays, tensors = {}, {}
    given = {name: _np.ascontiguousarray(inputs[name]) for name in _INS}
    given["vec_rows"] = _np.concatenate([_np.asarray(inputs[n]).reshape(-1, P) for n in
                                         ("c", "c_2", "norm_g", "norm_g_2", "gm_bs_2")])
    given["table"] = table()
    for name, a in given.items():
        arrays[f"in_{name}"] = a
        tensors[name] = nc.dram_tensor(f"in_{name}", a.shape, mybir.dt.from_np(a.dtype), kind="ExternalInput").ap()
    out = nc.dram_tensor("out", (1, S, D), F32, kind="ExternalOutput").ap()
    build(nc, tensors, out)
    r = _run(nc, [arrays], core_ids=[0])
    return r.results[0]["out"]
```

```python
import math
from contextlib import ExitStack

import concourse.bass as bass
from concourse import mybir

F32 = mybir.dt.float32
F32R = mybir.dt.float32r
I32 = mybir.dt.int32
ACT = mybir.ActivationFunctionType
ALU = mybir.AluOpType
AX = mybir.AxisListType.X

P = 128
S = 256
NT = S // P
D = 1024
ND = D // P
F = 2816
CF = 256
NF = F // CF
PIECE = 2048
RING = 3
ADA_RING = 2
START_RING = 5
ARENA = 13312
MODS = 9 * ND
EPS = 1e-6
NEG = -1e30
NCMP = (S - 32) // 16 + 1
LAMBDA_INIT = 0.8 - 0.6 * math.exp(-0.3)
TWO_PI = 2.0 * math.pi
PI_A = 6.28125
PI_B = math.floor((TWO_PI - PI_A) * 2 ** 19) / 2 ** 19
PI_C = TWO_PI - PI_A - PI_B

C_ID = 0
C_CAUSAL = C_ID + P
C_TRIL = C_CAUSAL + P
C_SCAN = C_TRIL + P
NLEVEL = 7
C_LEVEL = C_SCAN + 4 * S
C_CMPM = C_LEVEL + NLEVEL * P
C_CMPN = C_CMPM + NT * NCMP
C_COS = C_CMPN + NT * NCMP
C_SIN = C_COS + NT * 32
C_CCOS = C_SIN + NT * 32
C_CSIN = C_CCOS + 32
C_FREQ = C_CSIN + 32
C_END = C_FREQ + 8
N_CONST = 7
N_LATE = 6


class Tally:

    def __init__(self, **credits):
        self.n, self.i, self.per = dict(credits), None, {}

    def next(self, sem, by=1):
        name = label(sem)
        self.n[name] = self.n.get(name, 0) + by
        per = self.per.get(name, 0) if self.i is not None else 0
        return self.i * per + self.n[name] if per else self.n[name]

    def enter(self, i, per):
        self.i, self.per, self.before = i, {label(s): k for s, k in per}, dict(self.n)

    def leave(self, turns):
        for name in self.n:
            before, per = self.before.get(name, 0), self.per.get(name, 0)
            assert self.n[name] - before == per, (name, self.n[name] - before, per)
            self.n[name] = before + turns * per
        self.i, self.per = None, {}


def label(sem):
    return sem if isinstance(sem, str) else sem.name


def bc(ap, shape):
    return ap.broadcast_to(shape)


def build(nc, T, out, upto=99):
    with ExitStack() as ctx:
        def sb(name, shape, dt=F32):
            return ctx.enter_context(nc.sbuf_tensor(name, shape, dt))

        def sem(name):
            return ctx.enter_context(nc.semaphore(name))

        PY = ctx.enter_context(nc.psum_tensor("PY", [P, 4, 512], F32))
        GU = ctx.enter_context(nc.psum_tensor("GU", [P, 2, 512], F32))
        TM = ctx.enter_context(nc.psum_tensor("TM", [P, 2, 512], F32))
        PYt = PY[:, :, :].rearrange("p b (d s) -> p (b d) s", d=2)

        raw = sb("raw", [P, RING, PIECE])
        wH = sb("wH", [P, RING, PIECE], F32R)
        wL = sb("wL", [P, RING, PIECE], F32R)
        ada = sb("ada", [P, ADA_RING, PIECE])
        acc = sb("acc", [P, 512])
        x = sb("x", [P, NT, D])
        xn = sb("xn", [P, NT, D])
        xH = sb("xH", [P, ND, S], F32R)
        xL = sb("xL", [P, ND, S], F32R)
        hH = sb("hH", [P, 2, S], F32R)
        hL = sb("hL", [P, 2, S], F32R)
        sh = sb("sh", [P, 2, NT, CF])
        gB = sb("gB", [P, D])
        cst = sb("cst", [P, C_END])
        rows = sb("rows", [P, 6, P])
        cols = sb("cols", [P, P])
        bT = sb("bT", [P, 4 * MODS])
        mod = sb("mod", [P, 4 * MODS])
        cs = sb("cs", [P, 2 * ND])
        vb = sb("vb", [P, 5 * P])
        posi = sb("posi", [P, NT], I32)
        posf = sb("posf", [P, NT])
        turns_i = sb("turns_i", [P, NT, 8], I32)
        turns_f = sb("turns_f", [P, NT, 8])
        ang = sb("ang", [P, 2, NT, 8])
        wrap = sb("wrap", [P, 2, NT, 8])
        lam = sb("lam", [P, 8])
        ones = sb("ones", [P, 1])
        st = sb("st", [P, 8])
        rstd = sb("rstd", [P, NT])
        scl = sb("scl", [P, ND])
        gcol = sb("gcol", [P, ND])
        M = sb("M", [P, ARENA])
        modf = M[:, 0:2 * D].rearrange("p (t d s) -> p t d s", t=NT, d=ND)
        diag = M[:, 2 * D:2 * D + NT * P].rearrange("p (t s) -> p t s", t=NT)
        start_ = [M[:, ARENA - (n + 1) * PIECE:ARENA - n * PIECE] for n in range(START_RING)]
        PT = PY[:, :, :].rearrange("p (t b) (d s) -> p t (b d) s", t=NT, s=P)
        xH2 = xH[:, :, :].rearrange("p (b d) s -> p b (d s)", d=2)
        xL2 = xL[:, :, :].rearrange("p (b d) s -> p b (d s)", d=2)
        ident = cst[:, C_ID:C_ID + P]
        shf = sh[:, :, :, :].rearrange("p a t f -> p (a t f)")

        k_, q_, b_ = (M[:, n * D:(n + 1) * D] for n in range(3))
        E = [M[:, n * D:(n + 1) * D] for n in (3, 4, 5)]
        att = M[:, 6 * D:7 * D].rearrange("p (h s) -> p h s", s=P)
        attX = M[:, 7 * D:7 * D + 512].rearrange("p (h s) -> p h s", s=P)
        v_ = M[:, 7 * D + 512:9 * D + 512].rearrange("p (t n) -> p t n", t=NT)
        g_ = M[:, 9 * D + 512:11 * D + 512].rearrange("p (t n) -> p t n", t=NT)
        qk_, sq_ = M[:, 0:D], M[:, D:2 * D]
        qT = M[:, 2 * D:4 * D].rearrange("p (h s) -> p h s", s=S)
        kT = M[:, 4 * D:6 * D].rearrange("p (h s) -> p h s", s=S)
        vB = M[:, 6 * D:8 * D].rearrange("p (t n) -> p t n", t=NT)
        p_ = [M[:, n * D:(n + 1) * D].rearrange("p (m s) -> p m s", s=S) for n in (8, 9)]
        a_ = [M[:, (20 + n) * 512:(21 + n) * 512].rearrange("p (h s) -> p h s", s=S) for n in range(2)]
        aT = [M[:, (22 + n) * 512:(23 + n) * 512] for n in range(2)]
        rot = M[:, 24 * 512:25 * 512].rearrange("p (n t g d) -> p n t g d", n=4, t=NT, g=8)
        on_ = [M[:, n * D:(n + 1) * D] for n in range(NT)]
        v2_ = M[:, 0:512].rearrange("p (b t n) -> p b t n", b=2, t=NT)
        qT2 = M[:, 512:1536].rearrange("p (h s) -> p h s", s=S)
        kT2 = M[:, 1536:2560].rearrange("p (b g s) -> p b g s", b=2, g=2)
        kcT = M[:, 2560:2592].rearrange("p (g n) -> p g n", g=2)
        vc_ = M[:, 2592:2720].rearrange("p (g n) -> p g n", g=2)
        gates = M[:, 2720:2768].rearrange("p (t h c b) -> p t h c b", t=NT, h=4, c=2)
        pc_ = M[:, 2768:3008].rearrange("p (c m n) -> p c m n", c=2, n=NCMP)
        pcf = M[:, 2768:3008].rearrange("p (m n) -> p m n", n=NCMP)
        kd_ = M[:, 3072:4096].rearrange("p (b t g c n) -> p b t g c n", b=2, t=NT, g=2, c=2)
        cT_ = M[:, 4096:5120].rearrange("p (j g s) -> p j g s", j=2, g=2)
        w1_ = [M[:, 5120:7168], M[:, 8192:10240]]
        rt_ = M[:, 7168:8192]
        a2_ = [M[:, n:n + D].rearrange("p (m s) -> p m s", s=S) for n in (3072, 4096)]
        aT2 = [M[:, n:n + D] for n in (5120, 6144)]
        yo_ = M[:, 7168:8192].rearrange("p (t n) -> p t n", t=NT)
        u_ = M[:, 8192:9216].rearrange("p (t n) -> p t n", t=NT)
        vg_ = M[:, 9216:10240].rearrange("p (t n) -> p t n", t=NT)
        ws_ = M[:, 10240:11264].rearrange("p (g s) -> p g s", s=P)
        wsT = M[:, 11264:12288]
        yT = wsT
        ln_ = M[:, 12288:13312].rearrange("p (a n) -> p a n", a=2)
        cd_ = xn[:, 0, :].rearrange("p (t m c n) -> p t m c n", t=NT, m=4, c=2)
        qr_ = xn[:, 1, :].rearrange("p (t n) -> p t n", t=NT)
        y_ = shf.rearrange("p (t n) -> p t n", t=NT)
        sg_ = [ada[:, n, :].rearrange("p (t n) -> p t n", t=NT) for n in range(2)]
        w2_ = sb("w2_", [P, 2, 64])
        peT = sb("peT", [P, 64])
        pec = sb("pec", [P, 2])
        hc_ = sb("hc_", [P, 2, 30])
        kct = rt_[:, 0:256].rearrange("p (n g d) -> p n g d", n=4, g=2)
        kcd = rt_[:, 256:512].rearrange("p (g c n) -> p g c n", g=2, c=2)
        bn_ = sb("bn_", [P, NT, 6])
        mv_ = sb("mv_", [P, NT, 2])
        C_ = lambda at, n: cst[:, at:at + n]
        cos2 = C_(C_COS, NT * 32).rearrange("p (t n) -> p t n", t=NT)
        sin2 = C_(C_SIN, NT * 32).rearrange("p (t n) -> p t n", t=NT)
        stu = sb("stu", [P, 2, 16])
        causal = cst[:, C_CAUSAL:C_CAUSAL + P]
        st8 = sb("st8", [P, 4, 32])
        GUf = GU[:, :, :].rearrange("p b n -> p (b n)")
        PAf = PY[:, 0:2, :].rearrange("p b n -> p (b n)")
        PBf = PY[:, 2:4, :].rearrange("p b n -> p (b n)")
        TMf = TM[:, :, :].rearrange("p b n -> p (b n)")

        s_const = sem("s_const")
        s_in = sem("s_in")
        s_late = sem("s_late")
        s_ones = sem("s_ones")
        s_raw = [sem(f"s_raw{i}") for i in range(RING)]
        s_high = sem("s_high")
        s_split = sem("s_split")
        s_eaten = sem("s_eaten")
        s_ada = [sem(f"s_ada{i}") for i in range(ADA_RING)]
        s_start = [sem(f"s_start{i}") for i in range(START_RING)]
        s_startfree = sem("s_startfree")
        s_adafree = sem("s_adafree")
        s_direct = sem("s_direct")
        s_acc = sem("s_acc")
        s_modp = sem("s_modp")
        s_dve = sem("s_dve")
        s_act = sem("s_act")
        s_col = sem("s_col")
        s_cs = sem("s_cs")
        s_x = sem("s_x")
        s_ss = sem("s_ss")
        s_var = sem("s_var")
        s_sd = sem("s_sd")
        s_y = sem("s_y")
        s_xn = sem("s_xn")
        s_xt = sem("s_xt")
        s_modf0 = sem("s_modf0")
        s_modf1 = sem("s_modf1")
        s_xh = sem("s_xh")
        s_xl = sem("s_xl")
        s_scl = sem("s_scl")
        s_gcol = sem("s_gcol")
        s_gp = sem("s_gp")
        s_gb = sem("s_gb")
        s_silu = sem("s_silu")
        s_h = sem("s_h")
        s_ht = sem("s_ht")
        s_hh = sem("s_hh")
        s_hl = sem("s_hl")
        s_out = sem("s_out")
        s_readA = sem("s_readA")
        s_readD = sem("s_readD")
        s_key = sem("s_key")
        s_sigq = sem("s_sigq")
        s_ln = sem("s_ln")
        s_expo = sem("s_expo")
        s_decay = sem("s_decay")
        s_z = sem("s_z")
        s_gram = sem("s_gram")
        s_sel = sem("s_sel")
        s_o = sem("s_o")
        s_sq = sem("s_sq")
        s_hvar = sem("s_hvar")
        s_hsd = sem("s_hsd")
        s_w1 = sem("s_w1")
        s_gm = sem("s_gm")
        s_gate = sem("s_gate")
        s_cmp = sem("s_cmp")
        s_hc = sem("s_hc")
        s_kc = sem("s_kc")
        s_wm = sem("s_wm")
        s_bnv = sem("s_bnv")
        s_bns = sem("s_bns")
        s_vn = sem("s_vn")
        s_sv = sem("s_sv")
        s_yb = sem("s_yb")
        s_cx = sem("s_cx")
        s_ce = sem("s_ce")
        s_pc = sem("s_pc")
        s_trig = sem("s_trig")
        s_trigd = sem("s_trigd")
        s_score = sem("s_score")
        s_scored = sem("s_scored")
        s_max = sem("s_max")
        s_exp = sem("s_exp")
        s_a = sem("s_a")
        s_at = sem("s_at")
        s_aT = sem("s_aT")
        s_merged = sem("s_merged")
        s_on = sem("s_on")
        s_ot = sem("s_ot")

        ONE = dict(ada="ada_w", wi="ffn_wi", wo="ffn_wo")
        TWO = dict(ada="ada_w_2", wi="ffn_w_in_2", wo="ffn_w_out_2")
        LAYERS = [(ONE, 0), (ONE, 1), (TWO, 0), (TWO, 1)]
        ADA_FIRST, ADA_REST = 8, 10

        PHASES = [(l, j) for l in range(4) for j in range(3)][:upto]
        PIECES = [20, 16, 26, 26]


        def ada_turns(l, j):
            if j == 0:
                return l, ADA_FIRST, ADA_REST
            return (l + 1, 0, ADA_FIRST) if l + 1 < len(LAYERS) else (l, 0, 0)

        MIX_CHUNKS = [(512, 512), (0, 512), (1024, 280), (1816, 512), (1304, 512), (2328, 512), (2840, 512),
                      (3352, 512), (3864, 512)]

        block = ctx.enter_context(nc.Block())

        @block.sync
        def _(sp):
            t = Tally()

            def load(view, k0, nk, lo, width):
                slot = t.next("piece") % RING
                sp.wait_ge(s_split, t.next(s_split))
                dst = raw[:, slot, 0:nk * width].rearrange("p (k n) -> p k n", k=nk)
                for q in range(2):
                    sp.dma_start(dst[:, q * nk // 2:(q + 1) * nk // 2, :],
                                 view[:, k0 + q * nk // 2:k0 + (q + 1) * nk // 2, lo:lo + width]
                                 ).then_inc(s_raw[slot], 16)

            def load_up(l, j, c, q):
                names, i = LAYERS[l]
                v = T[names["wi"]][i, j // 2].rearrange("(k p) (two f) -> p k two f", p=P, two=2)
                slot = t.next("piece") % RING
                sp.wait_ge(s_split, t.next(s_split))
                dst = raw[:, slot, :].rearrange("p (k two f) -> p k two f", k=4, two=2)
                for g in range(2):
                    sp.dma_start(dst[:, :, g, :], v[:, 4 * q:4 * q + 4, g, bass.ds(c * CF, CF)]
                                 ).then_inc(s_raw[slot], 16)

            def load_down(l, j, c):
                names, i = LAYERS[l]
                v = T[names["wo"]][i, j // 2].rearrange("(c k p) n -> c p k n", p=P, k=2)
                slot = t.next("piece") % RING
                sp.wait_ge(s_split, t.next(s_split))
                dst = raw[:, slot, :].rearrange("p (k n) -> p k n", k=2)
                for k in range(2):
                    sp.dma_start(dst[:, k, :], v[bass.ds(c, 1), :, k, :].rearrange("c p n -> p (c n)")
                                 ).then_inc(s_raw[slot], 16)

            def load_start(c, q):
                n = t.next("start")
                slot = n % START_RING
                if n > START_RING:
                    sp.wait_ge(s_startfree, n - START_RING)
                sp.dma_start(start_[slot].rearrange("p (k n) -> p k n", k=4),
                             T["ada_w"][0].rearrange("(k p) n -> p k n", p=P)[:, 4 * q:4 * q + 4,
                                                                              c * 512:(c + 1) * 512]
                             ).then_inc(s_start[slot], 16)

            def load_ada(l, c, q):
                names, i = LAYERS[l]
                v = T[names["ada"]][i].rearrange("(k p) n -> p k n", p=P)
                slot = t.next("ada") % ADA_RING
                sp.wait_ge(s_adafree, t.next(s_adafree))
                sp.dma_start(ada[:, slot, :].rearrange("p (k n) -> p k n", k=4),
                             v[:, 4 * q:4 * q + 4, bass.ds(c * 512, 512)]).then_inc(s_ada[slot], 16)

            def late_constants():
                sp.dma_start(cst[:, P:C_END], T["table"][:, P:C_END]).then_inc(s_late, 16)
                sp.dma_start(posi[:, :], T["positions"][0].rearrange("(t p) -> p t", p=P),
                             allow_slow_non_contiguous=True).then_inc(s_late, 16)
                for at, n, name in ((0, P, "a_onorm"), (P, P, "b_qk_g"), (2 * P, P, "b_subln"),
                                    (3 * P, 2 * P, "b_lam")):
                    sp.dma_start(vb[:, at:at + n], T[name].rearrange(
                        "a n -> (a n)" if len(T[name].shape) == 2 else "a b n -> (a b n)").unsqueeze(0).broadcast_to(
                        [P, n])).then_inc(s_late, 16)

            def ffn(l, j):
                load_up(l, j, 0, 0)
                load_up(l, j, 0, 1)
                if (l, j) == (0, 0):
                    late_constants()
                la, c0, turns = ada_turns(l, j)

                def loop(first, count, with_ada):
                    with sp.Fori(0, count) as i:
                        t.enter(i, [(s_split, 3), ("piece", 3), (s_adafree, 2 * with_ada), ("ada", 2 * with_ada)])
                        load_up(l, j, first + i, 0)
                        if with_ada and (l, j) == (2, 2):
                            sp.wait_ge(s_x, NT * (3 * l + 2))
                        if with_ada:
                            load_ada(la, c0 + i, 0)
                        load_up(l, j, first + i, 1)
                        if with_ada:
                            load_ada(la, c0 + i, 1)
                        load_down(l, j, first + i - 1)
                    t.leave(count)

                if turns:
                    loop(1, turns, 1)
                if turns < NF - 1:
                    loop(1 + turns, NF - 1 - turns, 0)
                load_down(l, j, NF - 1)

            sp.dma_start(rows[0:P, 0, :], T["vec_rows"]).then_inc(s_const, 16)
            sp.dma_start(ident, T["table"][:, C_ID:C_ID + P]).then_inc(s_const, 16)
            for l in range(4):
                sp.dma_start(rows[0:MODS, 1 + l, :], T["ada_b" if l < 2 else "ada_b_2"][l % 2].rearrange(
                    "(r n) -> r n", n=P)).then_inc(s_const, 16)
            sp.dma_start(rows[0:64, 5, :], T["cmp_pe_2"].rearrange("l j (k two) d -> (l j k) (two d)", two=2)
                         ).then_inc(s_const, 16)
            for c in range(ADA_FIRST):
                for q in range(2):
                    load_start(c, q)
                if c == 4:
                    sp.dma_start(x[:, :, :], T["x"][0].rearrange("(t p) d -> p t d", p=P)).then_inc(s_in, 16)
            for l, j in PHASES:
                if j != 1:
                    ffn(l, j)
                elif l == 0:
                    w = T["a_w_in"][0].rearrange("(k p) n -> p k n", p=P)
                    for lo in (2 * D, D, 0, 2 * D + 512, 3 * D, 3 * D + 512, D + 512, 512):
                        load(w, 0, 4, lo, 512)
                        load(w, 4, 4, lo, 512)
                    w = T["a_w_out"][0].rearrange("(k p) n -> p k n", p=P)
                    for q in range(2):
                        for h in range(2):
                            load(w, 4 * q, 4, h * 512, 512)
                elif l == 1:
                    for name, halves in (("b_w_in", 6), ("b_w_out", 2)):
                        w = T[name][0].rearrange("(k p) n -> p k n", p=P)
                        for h in range(halves):
                            load(w, 0, 4, h * 512, 512)
                            load(w, 4, 4, h * 512, 512)
                else:
                    i = l - 2
                    sp.wait_ge(s_x, NT * (3 * l - 1))
                    for k in range(2):
                        for two in range(2):
                            sp.dma_start(w1_[k].rearrange("p (l f) -> p l f", f=P)[two * 64:(two + 1) * 64],
                                         T["cmp_w1_2"][i, k].rearrange("(l two) d f -> two d l f", two=2)[two]
                                         ).then_inc(s_w1, 16)
                    sp.dma_start(w2_[:, :, :], T["cmp_w2_2"][i].rearrange("j f d -> f j d")).then_inc(s_w1, 16)
                    sp.dma_start(ws_, T["gm_ws_2"][i].rearrange("g t s -> t g s")).then_inc(s_gm, 16)
                    for k, name in enumerate(("gm_ln_g_2", "gm_ln_b_2")):
                        sp.dma_start(ln_[:, k, :], T[name][i].unsqueeze(0).broadcast_to([P, 512])).then_inc(s_gm, 16)
                    w = T["mix_w_in_2"][i].rearrange("(k p) n -> p k n", p=P)
                    for lo, width in MIX_CHUNKS:
                        load(w, 0, 4, lo, width)
                        load(w, 4, 4, lo, width)
                    for h in range(2):
                        for name in ("proj_a_2", "proj_b_2"):
                            load(T[name][i].rearrange("(k p) n -> p k n", p=P), 0, 4, h * 512, 512)
                    w = T["w_out_2"][i].rearrange("(k p) n -> p k n", p=P)
                    for q in range(2):
                        for h in range(2):
                            load(w, 4 * q, 4, h * 512, 512)
            if len(PHASES) == 12:
                sp.wait_ge(s_x, NT * 11)
                sp.dma_start(ln_, T["final_g_2"].unsqueeze(0).broadcast_to([P, D])
                             .rearrange("p (a n) -> p a n", a=2)).then_inc(s_late, 16)
            sp.wait_ge(s_x, NT * (len(PHASES) + (len(PHASES) == 12)))
            sp.dma_start(out[0].rearrange("(t p) d -> p t d", p=P), x[:, :, :]).then_inc(s_out, 16)
            sp.wait_ge(s_out, 16)

        @block.scalar
        def _(act):
            t = Tally(done=RING)

            def cut(words=PIECE):
                slot = t.next("piece") % RING
                act.wait_ge(s_raw[slot], t.next(s_raw[slot], 32))
                act.wait_ge(s_eaten, t.next(s_eaten))
                act.activation(wH[:, slot, 0:words], raw[:, slot, 0:words], ACT.Copy).then_inc(s_high, 1)

            def root_table():
                act.activation(st[:, 7:8], ones[:, :], ACT.Sqrt)

            def root(i, first=False):
                if first:
                    act.wait_ge(s_in, 16)
                else:
                    act.wait_ge(s_x, t.next(s_x))
                act.activation(xn[:, i, :], x[:, i, :], ACT.Square, accum_out=st[:, i:i + 1]).then_inc(s_ss, 1)
                act.wait_ge(s_var, t.next(s_var))
                act.activation(st[:, 4 + i:5 + i], st[:, 2 + i:3 + i], ACT.Sqrt).then_inc(s_sd, 1)

            def norm(l, j):
                m = (3 * l + j) * 3 * ND
                root_table()
                act.wait_ge(s_scl, t.next(s_scl))
                for i in range(NT):
                    root(i, (l, j) == PHASES[0])
                    if i == 0:
                        cut()
                    toks = slice(i * P, (i + 1) * P)

                    def high(b):
                        act.activation(xH[:, 2 * b:2 * b + 2, toks], modf[:, i, 2 * b:2 * b + 2, :],
                                       ACT.Copy).then_inc(s_xh, 1)

                    def modulate(b):
                        for d in (2 * b, 2 * b + 1):
                            ins = act.activation(modf[:, i, d, :], PT[:, i, d, :], ACT.Identity,
                                                 bias=mod[:, m + d:m + d + 1], scale=scl[:, d:d + 1])
                        ins.then_inc(s_modf1, 1)

                    act.wait_ge(s_modf0, t.next(s_modf0))
                    high(0)
                    act.wait_ge(s_xt, t.next(s_xt, 2))
                    modulate(2)
                    act.wait_ge(s_modf0, t.next(s_modf0))
                    high(1)
                    modulate(3)
                    act.wait_ge(s_modf1, t.next(s_modf1, 1))
                    high(2)
                    act.wait_ge(s_modf1, t.next(s_modf1, 1))
                    high(3)
                act.wait_ge(s_gp, t.next(s_gp))
                act.activation(gB[:, :], TMf, ACT.Copy).then_inc(s_gb, 1)

            def silu_gate():
                act.wait_ge(s_eaten, t.next("done", 2))
                act.activation(sh[:, 0, :, :], GU[:, :, 0:CF], ACT.Silu).then_inc(s_silu, 1)

            def hidden_high():
                act.wait_ge(s_ht, t.next(s_ht))
                act.activation(hH[:, :, :].rearrange("p f s -> p (f s)"), TM[:, 0, :], ACT.Copy).then_inc(s_hh, 1)

            def ffn(l, j):
                norm(l, j)
                silu_gate()

                def loop(count):
                    with act.Fori(0, count) as i:
                        t.enter(i, [("piece", 3), (s_eaten, 3), ("done", 3), (s_ht, 1)] + [(s, 32) for s in s_raw])
                        cut()
                        hidden_high()
                        cut()
                        cut()
                        silu_gate()
                        t.next("done")
                    t.leave(count)

                _, _, turns = ada_turns(l, j)
                if turns:
                    loop(turns)
                if turns < NF - 1:
                    loop(NF - 1 - turns)
                if (l, j) != PHASES[-1]:
                    cut()
                hidden_high()
                t.next("done")

            def head_norm(src, dst):
                act.wait_ge(s_o, t.next(s_o))
                act.activation(dst, src, ACT.Square).then_inc(s_sq, 1)

            def head_root(n):
                act.wait_ge(s_hvar, t.next(s_hvar))
                act.activation(st8[:, 1, 0:n], st8[:, 0, 0:n], ACT.Sqrt).then_inc(s_hsd, 1)

            def evacuate(dst, src, func=ACT.Copy):
                act.wait_ge(s_eaten, t.next("done", 2))
                act.activation(dst, src, func).then_inc(s_readA, 1)

            def chained(instruction):
                instruction.then_inc(s_act, 1)
                act.wait_ge(s_act, t.next(s_act))

            def high_out(dst, src):
                act.wait_ge(s_ot, t.next(s_ot))
                act.activation(dst, src, ACT.Copy).then_inc(s_xh, 1)

            def hgrn():
                norm(0, 1)
                cut()
                evacuate(v_[:, :, 0:512], GU[:, :, :])
                cut()
                cut()
                for grp in range(2):
                    forget, query = (GUf, PAf) if grp else (PAf, GUf)
                    act.wait_ge(s_eaten, t.next("done", 2))
                    act.activation(k_, forget, ACT.Sigmoid, scale=-1.0)
                    act.activation(E[0], forget, ACT.Abs).then_inc(s_key, 1)
                    if grp == 0:
                        cut()
                    act.wait_ge(s_eaten, t.next("done", 2))
                    act.activation(E[1], query, ACT.Sigmoid).then_inc(s_sigq, 1)
                    if grp == 0:
                        cut()
                    act.wait_ge(s_key, t.next(s_key))
                    chained(act.activation(E[0], E[0], ACT.Exp, scale=-1.0))
                    act.activation(E[0], E[0], ACT.Ln, bias=1.0).then_inc(s_ln, 1)
                    if grp == 0:
                        cut()
                        cut()
                        evacuate(v_[:, :, 512:D], PY[:, 0:2, :])
                    for n in range(9):
                        if n < 8:
                            act.wait_ge(s_expo, t.next(s_expo))
                            e = E[(n + 1) % 3]
                            act.activation(e, e, ACT.Exp).then_inc(s_decay, 1)
                        if grp == 0 and n < 6 or grp == 1 and n in (6, 8):
                            cut()
                        if grp == 0 and n == 3:
                            evacuate(g_[:, :, 0:512], GU[:, :, :], ACT.Silu)
                        if grp == 0 and n == 5:
                            evacuate(g_[:, :, 512:D], PY[:, 0:2, :], ACT.Silu)
                    head_norm(TMf, E[0])
                    head_root(8)
                    high_out(xH[:, 4 * grp:4 * grp + 4, :].rearrange("p d s -> p (d s)"), GUf if grp else PBf)
                cut()
                cut()
                t.next("done", 4)

            def high_bank(b):
                act.wait_ge(s_ot, t.next(s_ot))
                act.activation(xH2[:, b, :], PY[:, b, :], ACT.Copy).then_inc(s_xh, 1)

            def exponentials(u, width):
                act.wait_ge(s_max, t.next(s_max))
                for m in range(4):
                    ins = act.activation(p_[u % 2][:, m, 0:width], p_[u % 2][:, m, 0:width], ACT.Exp,
                                         bias=stu[:, u % 2, m:m + 1], accum_out=stu[:, u % 2, 4 + m:5 + m])
                ins.then_inc(s_exp, 1)

            def weights_out(u, width):
                act.wait_ge(s_at, t.next(s_at))
                act.activation(aT[u % 2][:, 0:width], TM[:, u % 2, 0:width], ACT.Copy).then_inc(s_aT, 1)

            def diff():
                norm(1, 1)
                cut()
                act.wait_ge(s_trig, 1)
                act.activation(lam[:, 2:4], lam[:, 0:2], ACT.Exp)
                act.activation(ang[:, :, :, :].rearrange("p a t n -> p (a t n)"),
                               ang[:, :, :, :].rearrange("p a t n -> p (a t n)"), ACT.Sin).then_inc(s_trigd, 1)
                for c in range(4):
                    banks = GUf if c % 2 == 0 else PAf
                    act.wait_ge(s_eaten, t.next("done", 2))
                    act.activation(sq_, banks, ACT.Square).then_inc(s_sq, 1)
                    head_root(16)
                    cut()
                    cut()
                    act.wait_ge(s_ot, t.next(s_ot))
                    dst = (qT if c < 2 else kT)[:, 4 * (c % 2):4 * (c % 2) + 4, :].rearrange("p h s -> p (h s)")
                    act.activation(dst, TMf, ACT.Copy).then_inc(s_aT, 1)
                evacuate(vB[:, :, 0:512], GU[:, :, :])
                cut()
                exponentials(0, P)
                evacuate(vB[:, :, 512:D], PY[:, 0:2, :])
                cut()
                for u in range(8):
                    if u < 7:
                        exponentials(u + 1, P * ((u + 1) // 4 + 1))
                    weights_out(u, S * (u // 4 + 1))
                    if u == 4:
                        head_norm(GUf, xn[:, 0, :])
                        head_root(8)
                head_norm(GUf, xn[:, 0, :])
                head_root(8)
                for b in range(4):
                    high_bank(b)
                cut()
                cut()
                t.next("done", 4)

            def turned(dst, src):
                act.wait_ge(s_ot, t.next(s_ot))
                act.activation(dst, src, ACT.Copy).then_inc(s_aT, 1)

            def nsa(l):
                norm(l, 1)
                cut()
                cut(4 * 280)
                cut(4 * 280)
                act.wait_ge(s_ot, t.next(s_ot))
                src = TMf.rearrange("p (m s) -> p m s", s=S)
                dst = cT_.rearrange("p j g s -> p (j g) s")
                act.activation(dst[0:64], src[0:64], ACT.Copy)
                act.activation(dst[64:P, :, 0:S - 1], src[64:P, :, 1:S], ACT.Copy).then_inc(s_aT, 1)
                cut()
                cut()
                act.wait_ge(s_eaten, t.next("done", 6))
                act.activation(gates.rearrange("p t h c b -> p t (h c b)"), GU[:, :, 256:280],
                               ACT.Sigmoid).then_inc(s_gate, 1)
                turned(qT2.rearrange("p h s -> p (h s)"), TMf)
                act.wait_ge(s_cmp, t.next(s_cmp))
                t.next(s_cmp, 3)
                for k in range(2):
                    chained(act.activation(pec[:, k:k + 1], PY[:, 2, 64 * k + 32:64 * k + 33], ACT.Copy))
                    ins = act.activation(hc_[:, k, :], PY[:, 2, 64 * k:64 * k + 30], ACT.Silu, bias=pec[:, k:k + 1])
                ins.then_inc(s_hc, 1)
                cut()
                cut()
                evacuate(vg_, PY[:, 0:2, :], ACT.Gelu_apprx_tanh)
                act.wait_ge(s_bnv, t.next(s_bnv))
                act.activation(mv_[:, :, 1], mv_[:, :, 1], ACT.Sqrt).then_inc(s_bns, 1)
                turned(kT2.rearrange("p b g s -> p (b g s)"), TMf)
                cut()
                cut()
                evacuate(u_, GU[:, :, :], ACT.Gelu_apprx_tanh)
                turned(wsT, TMf)
                cut()
                cut()
                turned(yT, PBf)
                act.wait_ge(s_cx, t.next(s_cx))
                act.activation(pcf, pcf, ACT.Exp).then_inc(s_ce, 1)
                exponentials(0, P)
                evacuate(sg_[0][:, :, 0:512], PY[:, 0:2, :], ACT.Sigmoid)
                cut()
                for i in range(NT):
                    turned(xn[0:NCMP, i, :], TMf[0:NCMP])
                gates_out = {2: sg_[0][:, :, 512:D], 4: sg_[1][:, :, 0:512], 6: sg_[1][:, :, 512:D]}
                for u in range(8):
                    act.wait_ge(s_at, t.next(s_at))
                    if u // 4:
                        act.activation(aT2[u % 2], TMf, ACT.Copy).then_inc(s_aT, 1)
                    else:
                        act.activation(aT2[u % 2][:, 0:512], TM[:, u % 2, :], ACT.Copy).then_inc(s_aT, 1)
                    if u < 7:
                        exponentials(u + 1, P * ((u + 1) // 4 + 1))
                    if u in gates_out:
                        evacuate(gates_out[u], PY[:, 0:2, :], ACT.Sigmoid)
                    if 1 <= u <= 6:
                        cut()
                    if u == 6:
                        act.activation(xH[:, 4:8, :].rearrange("p d s -> p (d s)"), yT, ACT.Copy).then_inc(s_xh, 1)
                    if u == 4:
                        act.wait_ge(s_o, t.next(s_o))
                        act.activation(yo_[:, 0, :], GU[:, 0, :], ACT.Copy).then_inc(s_readA, 1)
                act.wait_ge(s_o, t.next(s_o))
                act.activation(yo_[:, 1, :], GU[:, 1, :], ACT.Copy).then_inc(s_readA, 1)
                high_out(xH[:, 0:4, :].rearrange("p d s -> p (d s)"), PBf)
                cut()
                cut()
                high_out(xH[:, 0:4, :].rearrange("p d s -> p (d s)"), GUf)
                cut()
                cut()
                high_out(xH[:, 4:8, :].rearrange("p d s -> p (d s)"), TMf)
                cut()
                t.next("done", 8)

            act.wait_ge(s_col, 1)
            act.activation(cs[:, :], TM[:, 0, 0:2 * ND], ACT.Silu).then_inc(s_cs, 1)
            for n, (l, j) in enumerate(PHASES):
                for _ in range(2 if n == 0 or PHASES[n - 1][1] == 1 else 1):
                    cut()
                if j != 1:
                    ffn(l, j)
                elif l == 0:
                    hgrn()
                elif l == 1:
                    diff()
                else:
                    nsa(l)
            if len(PHASES) == 12:
                for i in range(NT):
                    root(i)

        @block.vector
        def _(dve):
            t = Tally(done=RING)

            def chained(instruction):
                instruction.then_inc(s_dve, 1)
                dve.wait_ge(s_dve, t.next(s_dve))

            def cut(words=PIECE):
                slot = t.next("piece") % RING
                dve.wait_ge(s_high, t.next(s_high))
                dve.tensor_tensor(wL[:, slot, 0:words], raw[:, slot, 0:words], wH[:, slot, 0:words],
                                  ALU.subtract).then_inc(s_split, 1)

            def start_products(q, direct):
                slot = t.next("start") % START_RING
                dve.wait_ge(s_start[slot], t.next(s_start[slot], 16))
                products(0, q, start_[slot], 4 - direct)
                dve.wait_ge(s_direct, t.next(s_direct))
                dve.sem_inc(s_startfree, 1)
                if q == 1:
                    dve.sem_inc(s_acc, 1)

            def ada_products(l, q):
                slot = t.next("ada") % ADA_RING
                dve.wait_ge(s_ada[slot], t.next(s_ada[slot], 16))
                products(l, q, ada[:, slot, :], 4)
                dve.sem_inc(s_adafree, 1)
                if q == 1:
                    dve.sem_inc(s_acc, 1)

            def products(l, q, piece, tiles):
                for k in range(tiles):
                    w = piece[:, k * 512:(k + 1) * 512]
                    c = cs[:, (l // 2) * ND + 4 * q + k:(l // 2) * ND + 4 * q + k + 1]
                    if q == 0 and k == 0:
                        ins = dve.tensor_scalar(acc[:, :], w, c, None, ALU.mult)
                    else:
                        ins = dve.scalar_tensor_tensor(acc[:, :], w, c, acc[:, :], ALU.mult, ALU.add)
                    chained(ins)

            def ada_store(l, c, bank=TM[:, 1, :]):
                dve.wait_ge(s_modp, t.next(s_modp))
                at = l * MODS + 4 * c
                chained(dve.tensor_tensor(mod[:, bass.ds(at, 4)], bank[:, 0:4], bT[:, bass.ds(at, 4)], ALU.add))

            def root(i):
                dve.wait_ge(s_ss, t.next(s_ss))
                dve.tensor_scalar(st[:, 2 + i:3 + i], st[:, i:i + 1], 1.0 / D, EPS, ALU.mult, ALU.add
                                  ).then_inc(s_var, 1)
                dve.wait_ge(s_sd, t.next(s_sd))
                chained(dve.reciprocal(rstd[:, i:i + 1], st[:, 4 + i:5 + i]))

            def columns(l, j):
                m = (3 * l + j) * 3 * ND
                g = 2 * ND + (3 * l + j) * ND
                factor = 0.5 if j != 1 else 1.0
                gate = mod[:, m + 2 * ND:m + 3 * ND]
                if l < 2:
                    chained(dve.tensor_scalar(gcol[:, :], gate, 1.0, factor, ALU.add, ALU.mult))
                else:
                    chained(dve.tensor_scalar(gcol[:, :], gate, factor, None, ALU.mult))
                dve.tensor_copy(shf.rearrange("p (d n) -> p d n", n=P),
                                bc(gcol[:, :].unsqueeze(2), [P, ND, P])).then_inc(s_gcol, 1)
                dve.scalar_tensor_tensor(scl[:, :], mod[:, m + ND:m + 2 * ND], 1.0, cols[:, g:g + ND],
                                         ALU.add, ALU.mult).then_inc(s_scl, 1)
                dve.wait_ge(s_scl, t.next(s_scl))

            def gated_output(i):
                chained(dve.tensor_tensor(xn[:, i, :], PY[:, 2 * i:2 * i + 2, :].rearrange("p b n -> p (b n)"),
                                          gB[:, :], ALU.mult))

            def add_output(i):
                dve.tensor_tensor(x[:, i, :], x[:, i, :], xn[:, i, :], ALU.add).then_inc(s_x, 1)

            def boundary(l, j, pieces):
                m = (3 * l + j) * 3 * ND
                columns(l, j)
                cut()
                if pieces:
                    dve.wait_ge(s_gb, t.next(s_gb))
                    dve.wait_ge(s_y, t.next(s_y))
                    gated_output(0)
                    add_output(0)
                for i in range(NT):
                    toks = slice(i * P, (i + 1) * P)
                    root(i)
                    dve.tensor_scalar(diag[:, i, :], ident, rstd[:, i:i + 1], None, ALU.mult).then_inc(s_xn, 1)
                    if pieces and i == 0:
                        dve.wait_ge(s_eaten, t.next("done", pieces))
                        gated_output(1)
                    dve.wait_ge(s_xt, t.next(s_xt))
                    for b in range(2):
                        for d in (2 * b, 2 * b + 1):
                            ins = dve.tensor_scalar(modf[:, i, d, :], PT[:, i, d, :], scl[:, d:d + 1],
                                                    mod[:, m + d:m + d + 1], ALU.mult, ALU.add)
                        ins.then_inc(s_modf0, 1)
                    t.next(s_xt)
                    for b in range(4):
                        dve.wait_ge(s_xh, t.next(s_xh))
                        dve.tensor_tensor(xL[:, 2 * b:2 * b + 2, toks], modf[:, i, 2 * b:2 * b + 2, :],
                                          xH[:, 2 * b:2 * b + 2, toks], ALU.subtract).then_inc(s_xl, 1)
                        if pieces and i == 0 and b == 1:
                            add_output(1)
                cut()

            def hidden():
                dve.wait_ge(s_silu, t.next(s_silu))
                dve.tensor_tensor(sh[:, 1, :, :], sh[:, 0, :, :], GU[:, :, CF:2 * CF], ALU.mult).then_inc(s_h, 1)

            def hidden_low():
                dve.wait_ge(s_hh, t.next(s_hh))
                dve.tensor_tensor(hL[:, :, :].rearrange("p f s -> p (f s)"), TM[:, 0, :],
                                  hH[:, :, :].rearrange("p f s -> p (f s)"), ALU.subtract).then_inc(s_hl, 1)

            def ffn(l, j):
                hidden()
                la, c0, turns = ada_turns(l, j)

                def loop(count, with_ada):
                    with dve.Fori(0, count) as i:
                        per = [("piece", 3), (s_high, 3), (s_silu, 1), (s_hh, 1)]
                        if with_ada:
                            per += [("ada", 2), (s_dve, 9), (s_modp, 1)] + [(s, 16) for s in s_ada]
                        t.enter(i, per)
                        cut()
                        if with_ada:
                            ada_products(la, 0)
                            ada_products(la, 1)
                        hidden_low()
                        cut()
                        cut()
                        hidden()
                        if with_ada:
                            ada_store(la, c0 + i)
                    t.leave(count)

                if turns:
                    loop(turns, 1)
                if turns < NF - 1:
                    loop(NF - 1 - turns, 0)
                if (l, j) != PHASES[-1]:
                    cut()
                hidden_low()

            def head_norm(src, groups, width, spread, sq):
                dve.wait_ge(s_sq, t.next(s_sq))
                chained(dve.tensor_reduce(st8[:, 2, 0:groups], sq, AX, ALU.add))
                dve.tensor_scalar(st8[:, 0, 0:groups], st8[:, 2, 0:groups], 1.0 / width, EPS,
                                  ALU.mult, ALU.add).then_inc(s_hvar, 1)
                dve.wait_ge(s_hsd, t.next(s_hsd))
                chained(dve.reciprocal(st8[:, 3, 0:groups], st8[:, 1, 0:groups]))
                chained(dve.tensor_tensor(spread, src, bc(st8[:, 3, 0:groups].unsqueeze(2), [P, groups, width]),
                                          ALU.mult))

            def low_out(dst, src, high):
                dve.wait_ge(s_xh, t.next(s_xh))
                dve.tensor_tensor(dst, src, high, ALU.subtract).then_inc(s_xl, 1)

            def exponents(n, e):
                if n < 8:
                    m = 1 << (n - 1)
                    b4, e4 = (a.rearrange("p (g two m) -> p g two m", two=2, m=m) for a in (b_, e))
                    shape = [P, 4 * S // (2 * m), m]
                    ref = bc(b4[:, :, 0, m - 1:m], shape)
                    if m < 64:
                        dve.tensor_tensor(e4[:, :, 1, :], b4[:, :, 1, :], ref, ALU.subtract)
                    else:
                        dve.tensor_copy(e4[:, :, 1, :], b4[:, :, 1, :])
                    dve.tensor_tensor(e4[:, :, 0, :], ref, b4[:, :, 0, :], ALU.subtract).then_inc(s_expo, 1)
                    return
                b4, e4 = (a.rearrange("p (h c m) -> p h c m", h=4, c=4) for a in (b_, e))
                chained(dve.tensor_tensor(e4[:, :, 0:2, :], bc(b4[:, :, 0:2, 63:64], [P, 4, 2, 64]), b4[:, :, 0:2, :],
                                          ALU.subtract))
                chained(dve.tensor_copy(e4[:, :, 2:4, :], b4[:, :, 2:4, :]))
                dve.tensor_tensor(e4[:, :, 0, :], e4[:, :, 0, :], bc(b4[:, :, 1, 63:64], [P, 4, 64]), ALU.add)
                dve.tensor_tensor(e4[:, :, 3, :], e4[:, :, 3, :], bc(b4[:, :, 2, 63:64], [P, 4, 64]),
                                  ALU.add).then_inc(s_expo, 1)

            def decayed(n, e):
                m = 1 << (n - 1)
                dve.wait_ge(s_decay, t.next(s_decay))
                e4, q4, k4 = (a.rearrange("p (g two m) -> p g two m", two=2, m=m) for a in (e, q_, k_))
                dve.tensor_tensor(e4[:, :, 1, :], e4[:, :, 1, :], q4[:, :, 1, :], ALU.mult)
                dve.tensor_tensor(e4[:, :, 0, :], e4[:, :, 0, :], k4[:, :, 0, :], ALU.mult).then_inc(s_z, 1)

            def select(n):
                dve.wait_ge(s_gram, t.next(s_gram))
                src = (PBf if n % 2 == 0 else TMf).rearrange("p (h s) -> p h s", s=P)
                if n == 0:
                    ins = dve.tensor_tensor(att, src, bc(ident.unsqueeze(1), [P, 8, P]), ALU.mult)
                elif n < 8:
                    mask = cst[:, C_LEVEL + (n - 1) * P:C_LEVEL + n * P].bitcast(I32)
                    ins = dve.copy_predicated(att, bc(mask.unsqueeze(1), [P, 8, P]), src)
                else:
                    ins = dve.tensor_copy(attX, src[:, 0:4, :])
                ins.then_inc(s_sel, 1)
                dve.wait_ge(s_sel, t.next(s_sel))

            def hgrn():
                dve.wait_ge(s_late, N_LATE * 16)
                cut()
                cut()
                cut()
                for grp in range(2):
                    forget, query = (GUf, PAf) if grp else (PAf, GUf)
                    dve.wait_ge(s_key, t.next(s_key))
                    dve.tensor_scalar(b_, forget, 0.0, None, ALU.min).then_inc(s_readD, 1)
                    if grp == 0:
                        cut()
                    dve.wait_ge(s_sigq, t.next(s_sigq))
                    dve.tensor_tensor(q_, E[1], query, ALU.mult).then_inc(s_readD, 1)
                    dve.wait_ge(s_readD, t.next(s_readD, 2))
                    if grp == 0:
                        cut()
                    dve.wait_ge(s_ln, t.next(s_ln))
                    chained(dve.tensor_tensor(E[1], b_, E[0], ALU.subtract))
                    chained(dve.tensor_tensor_scan(b_, cst[:, C_SCAN:C_SCAN + 4 * S], E[1], 0.0, ALU.mult, ALU.add))
                    if grp == 0:
                        cut()
                        cut()
                    for n in range(9):
                        if n < 8:
                            exponents(n + 1, E[(n + 1) % 3])
                        if n:
                            decayed(n, E[n % 3])
                            select(n - 1)
                        if grp == 0 and n < 6 or grp == 1 and n == 7:
                            cut()
                    select(8)
                    if grp == 1:
                        cut()
                    by_head = lambda a: a.rearrange("p (g n) -> p g n", n=P)
                    head_norm(by_head(TMf), 8, P, by_head(q_), by_head(E[0]))
                    chained(dve.tensor_tensor(by_head(q_), by_head(q_), bc(vb[:, 0:P].unsqueeze(1), [P, 8, P]),
                                              ALU.mult))
                    by_tile = q_.rearrange("p (t n) -> p t n", t=NT)
                    dve.tensor_tensor(by_tile, by_tile, g_[:, :, grp * 512:(grp + 1) * 512], ALU.mult
                                      ).then_inc(s_on, 1)
                    d = slice(4 * grp, 4 * grp + 4)
                    low_out(xL[:, d, :].rearrange("p d s -> p (d s)"), GUf if grp else PBf,
                            xH[:, d, :].rearrange("p d s -> p (d s)"))
                t.next(s_ot, 2)
                t.next(s_on, 2)
                t.next(s_readA, 4)
                cut()
                cut()

            def low_bank(b):
                dve.wait_ge(s_xh, t.next(s_xh))
                dve.tensor_tensor(xL2[:, b, :], PY[:, b, :], xH2[:, b, :], ALU.subtract).then_inc(s_xl, 1)

            def lambda_and_angles():
                prod = wrap[:, :, :, :].rearrange("p a t n -> p (a t n)")
                for n in range(2):
                    at = 3 * P + n * P
                    chained(dve.tensor_tensor(vb[:, at:at + 64], vb[:, at:at + 64], vb[:, at + 64:at + P], ALU.mult))
                    chained(dve.tensor_reduce(lam[:, n:n + 1], vb[:, at:at + 64], AX, ALU.add))
                chained(dve.tensor_scalar(vb[:, 2 * P:3 * P], vb[:, 2 * P:3 * P], 1.0 - LAMBDA_INIT, None, ALU.mult))
                chained(dve.tensor_copy(posf[:, :], posi[:, :]))
                raw_angle = ang[:, 0, :, :]
                chained(dve.tensor_tensor(raw_angle, bc(posf[:, :].unsqueeze(2), [P, NT, 8]),
                                          bc(cst[:, C_FREQ:C_FREQ + 8].unsqueeze(1), [P, NT, 8]), ALU.mult))
                chained(dve.tensor_scalar(turns_i[:, :, :], raw_angle, 1.0 / TWO_PI, None, ALU.mult))
                chained(dve.tensor_copy(turns_f[:, :, :], turns_i[:, :, :]))
                for part in (PI_A, PI_B, PI_C):
                    chained(dve.scalar_tensor_tensor(raw_angle, turns_f[:, :, :], -part, raw_angle,
                                                     ALU.mult, ALU.add))
                chained(dve.tensor_scalar(ang[:, 1, :, :], raw_angle, TWO_PI / 4, None, ALU.add))
                flat = ang[:, :, :, :].rearrange("p a t n -> p (a t n)")
                for op, edge, by in ((ALU.is_gt, TWO_PI / 2, -TWO_PI), (ALU.is_lt, -TWO_PI / 2, TWO_PI)):
                    chained(dve.tensor_scalar(prod, flat, edge, by, op, ALU.mult))
                    chained(dve.tensor_tensor(flat, flat, prod, ALU.add))
                dve.tensor_scalar(flat, flat, -3.1415925, 3.1415925, ALU.max, ALU.min).then_inc(s_trig, 1)
                dve.wait_ge(s_trigd, 1)
                chained(dve.tensor_tensor(lam[:, 4:5], lam[:, 3:4], lam[:, 2:3], ALU.subtract))
                chained(dve.tensor_scalar(lam[:, 5:6], lam[:, 4:5], LAMBDA_INIT, None, ALU.subtract))

            def mask_and_max(u, tile, banks):
                dve.wait_ge(s_score, t.next(s_score))
                src, dst, width = banks.rearrange("p (m s) -> p m s", s=S), p_[u % 2], P * (tile + 1)
                if tile:
                    dve.tensor_scalar(dst[:, :, 0:P], src[:, :, 0:P], 0.125, None, ALU.mult)
                dve.scalar_tensor_tensor(dst[:, :, tile * P:width], src[:, :, tile * P:width], 0.125,
                                         bc(causal.unsqueeze(1), [P, 4, P]), ALU.mult, ALU.add).then_inc(s_scored, 1)
                dve.wait_ge(s_scored, t.next(s_scored))
                chained(dve.tensor_reduce(stu[:, u % 2, 8:12], dst[:, :, 0:width], AX, ALU.max))
                dve.tensor_scalar(stu[:, u % 2, 0:4], stu[:, u % 2, 8:12], -1.0, None, ALU.mult).then_inc(s_max, 1)

            def difference(u, tile):
                width, stt = P * (tile + 1), stu[:, u % 2, :]
                dve.wait_ge(s_exp, t.next(s_exp))
                chained(dve.reciprocal(stt[:, 8:12], stt[:, 4:8]))
                chained(dve.tensor_scalar(stt[:, 12:14], stt[:, 10:12], lam[:, 5:6], None, ALU.mult))
                if u > 1:
                    dve.wait_ge(s_at, t.next(s_at))
                for h in range(2):
                    ins = dve.tensor_scalar(a_[u % 2][:, h, 0:width], p_[u % 2][:, h, 0:width], stt[:, 8 + h:9 + h],
                                            None, ALU.mult)
                chained(ins)
                for h in range(2):
                    ins = dve.scalar_tensor_tensor(a_[u % 2][:, h, 0:width], p_[u % 2][:, 2 + h, 0:width],
                                                   stt[:, 12 + h:13 + h], a_[u % 2][:, h, 0:width],
                                                   ALU.mult, ALU.add)
                ins.then_inc(s_a, 1)

            def rotate(x1, x2, cos, sin, y1, y2, tmp):
                dve.tensor_tensor(tmp[0], x1, cos, ALU.mult)
                dve.tensor_tensor(tmp[1], x2, sin, ALU.mult)
                dve.tensor_tensor(tmp[2], x2, cos, ALU.mult)
                chained(dve.tensor_tensor(tmp[3], x1, sin, ALU.mult))
                dve.tensor_tensor(y1, tmp[0], tmp[1], ALU.subtract)
                return dve.tensor_tensor(y2, tmp[2], tmp[3], ALU.add)

            def diff():
                lambda_and_angles()
                cut()
                q16 = qk_.rearrange("p (g n) -> p g n", n=64)
                q4 = qk_.rearrange("p (t g n) -> p t g n", t=NT, n=64)
                shape = [P, NT, 8, 8]
                for c in range(4):
                    banks = GUf if c % 2 == 0 else PAf
                    if c:
                        dve.wait_ge(s_ot, t.next(s_ot))
                    head_norm(banks.rearrange("p (g n) -> p g n", n=64), 16, 64, q16,
                              sq_.rearrange("p (g n) -> p g n", n=64))
                    dve.sem_inc(s_readD, 1)
                    g = vb[:, P + (c // 2) * 64:P + (c // 2 + 1) * 64]
                    chained(dve.tensor_tensor(q16, q16, bc(g.unsqueeze(1), [P, 16, 64]), ALU.mult))
                    rotate(q4[:, :, :, 0:8], q4[:, :, :, 8:16], bc(ang[:, 1, :, :].unsqueeze(2), shape),
                           bc(ang[:, 0, :, :].unsqueeze(2), shape), q4[:, :, :, 0:8], q4[:, :, :, 8:16],
                           [rot[:, n] for n in range(4)]).then_inc(s_on, 1)
                    cut()
                    cut()
                t.next(s_ot)
                cut()
                mask_and_max(0, 0, PBf)
                for u in range(8):
                    if u < 7:
                        mask_and_max(u + 1, (u + 1) // 4, PBf if u % 2 else PAf)
                    difference(u, u // 4)
                    if u == 0:
                        cut()
                    if u == 4:
                        out_norm(0)
                out_norm(1)
                for b in range(4):
                    low_bank(b)
                t.next(s_at, 2)
                t.next(s_ot, 4)
                t.next(s_on, 6)
                t.next(s_readA, 2)
                cut()
                cut()

            def keys_rotated(src, branch):
                x4 = src.rearrange("p t (g n) -> p t g n", g=2)
                shape, d = [P, NT, 2, 32], kd_[:, branch]
                tmp = [rt_[:, n * P:(n + 1) * P].rearrange("p (t g n) -> p t g n", t=NT, g=2) for n in range(4)]
                chained(rotate(x4[:, :, :, 0:32], x4[:, :, :, 32:64], bc(cos2.unsqueeze(2), shape),
                               bc(sin2.unsqueeze(2), shape), d[:, :, :, 0, 0:32], d[:, :, :, 0, 32:64], tmp))
                return dve.tensor_copy(d[:, :, :, 1, :], d[:, :, :, 0, :])

            def gated(u, tile):
                width, stt = P * (tile + 1), stu[:, u % 2, :]
                g, b = u // 2 % 2, u % 2
                dve.wait_ge(s_exp, t.next(s_exp))
                chained(dve.reciprocal(stt[:, 8:12], stt[:, 4:8]))
                gate = gates[:, tile, 2 * g:2 * g + 2, :, 1 + b].rearrange("p h c -> p c h")
                pairs = lambda a: a.rearrange("p (c h) -> p c h", c=2)
                chained(dve.tensor_tensor(pairs(stt[:, 12:16]), pairs(stt[:, 8:12]), gate, ALU.mult))
                if u > 1:
                    dve.wait_ge(s_at, t.next(s_at))
                for m in range(4):
                    ins = dve.tensor_scalar(a2_[u % 2][:, m, 0:width], p_[u % 2][:, m, 0:width],
                                            stt[:, 12 + m:13 + m], None, ALU.mult)
                ins.then_inc(s_a, 1)

            def nsa(l):
                cut()
                dve.wait_ge(s_eaten, t.next("done", 2))
                for i in range(NT):
                    dve.tensor_copy(cd_[:, i], bc(GU[:, i, 0:256].rearrange("p (m n) -> p m n", n=64).unsqueeze(2),
                                                  [P, 4, 2, 64]))
                dve.tensor_copy(v2_[:, 0], GU[:, :, 384:512])
                keys_rotated(GU[:, :, 256:384], 0).then_inc(s_on, 1)
                dve.wait_ge(s_on, t.next(s_on))
                dve.sem_inc(s_readD, 1)
                cut(4 * 280)
                cut(4 * 280)
                dve.wait_ge(s_eaten, t.next("done", 2))
                for i in range(NT):
                    x3 = PY[:, i, :].rearrange("p (h n) -> p h n", n=64)
                    y3 = qr_[:, i, :].rearrange("p (h n) -> p h n", n=64)
                    tmp = [rt_[:, n * S:(n + 1) * S].rearrange("p (h n) -> p h n", n=32) for n in range(4)]
                    ins = rotate(x3[:, :, 0:32], x3[:, :, 32:64], bc(cos2[:, i:i + 1, :], [P, 8, 32]),
                                 bc(sin2[:, i:i + 1, :], [P, 8, 32]), y3[:, :, 0:32], y3[:, :, 32:64], tmp)
                    if i == 0:
                        chained(ins)
                ins.then_inc(s_on, 1)
                dve.wait_ge(s_on, t.next(s_on))
                dve.sem_inc(s_readD, 1)
                cut()
                cut()
                dve.wait_ge(s_gate, t.next(s_gate))
                t.next("done", 2)
                dve.tensor_copy(v2_[:, 1], GU[:, :, 128:256])
                keys_rotated(GU[:, :, 0:128], 1).then_inc(s_on, 1)
                dve.wait_ge(s_on, t.next(s_on))
                dve.sem_inc(s_readD, 1)
                cut()
                cut()
                dve.wait_ge(s_cmp, t.next(s_cmp, 2))
                kv = PY[0:NCMP, 3, 0:256].rearrange("p (m n) -> p m n", n=64)
                dve.tensor_copy(vc_[0:NCMP], kv[:, 2:4, :])
                shape = [NCMP, 2, 32]
                chained(rotate(kv[:, 0:2, 0:32], kv[:, 0:2, 32:64],
                               bc(cst[0:NCMP, C_CCOS:C_CCOS + 32].unsqueeze(1), shape),
                               bc(cst[0:NCMP, C_CSIN:C_CSIN + 32].unsqueeze(1), shape),
                               kcd[0:NCMP, :, 0, 0:32], kcd[0:NCMP, :, 0, 32:64], [kct[0:NCMP, n] for n in range(4)]))
                dve.tensor_copy(kcd[0:NCMP, :, 1, :], kcd[0:NCMP, :, 0, :]).then_inc(s_kc, 1)
                dve.wait_ge(s_gm, 48 * (l - 1))
                dve.tensor_tensor(ws_, ws_, bc(cst[:, C_TRIL:C_TRIL + P].unsqueeze(1), [P, 8, P]),
                                  ALU.mult).then_inc(s_wm, 1)
                dve.wait_ge(s_readA, t.next(s_readA))
                for i in range(NT):
                    chained(dve.bn_stats(bn_[:, i, :], vg_[:, i, :]))
                for i in range(NT):
                    chained(dve.bn_aggr(mv_[:, i, :], bn_[:, i, :]))
                dve.tensor_scalar(mv_[:, :, 1], mv_[:, :, 1], EPS, None, ALU.add).then_inc(s_bnv, 1)
                cut()
                cut()
                dve.wait_ge(s_bns, t.next(s_bns))
                chained(dve.reciprocal(mv_[:, :, 1], mv_[:, :, 1]))
                for i in range(NT):
                    ins = dve.tensor_scalar(vg_[:, i, :], vg_[:, i, :], mv_[:, i, 0:1], mv_[:, i, 1:2],
                                            ALU.subtract, ALU.mult)
                chained(ins)
                chained(dve.tensor_tensor(vg_, vg_, bc(ln_[:, 0:1, :], [P, NT, 512]), ALU.mult))
                dve.tensor_tensor(vg_, vg_, bc(ln_[:, 1:2, :], [P, NT, 512]), ALU.add).then_inc(s_vn, 1)
                dve.wait_ge(s_cmp, t.next(s_cmp))
                dve.tensor_copy(kcT[:, :, 0:NCMP], PY[:, 2, 0:32].rearrange("p (g n) -> p g n", g=2)[:, :, 0:NCMP]
                                ).then_inc(s_kc, 1)
                cut()
                dve.wait_ge(s_sv, t.next(s_sv))
                y4, u4, p4 = (a.rearrange("p t (g n) -> p t g n", n=64) for a in (y_, u_, PY[:, 2:4, :]))
                at = 2 * ND + 12 * ND + (l - 2) * 8
                chained(dve.tensor_tensor(y4, p4, bc(cols[:, at:at + 8].unsqueeze(1).unsqueeze(3), [P, NT, 8, 64]),
                                          ALU.add))
                dve.tensor_tensor(y4, y4, u4, ALU.mult).then_inc(s_yb, 1)
                cut()
                dve.wait_ge(s_cmp, t.next(s_cmp))
                for c in range(2):
                    for i in range(NT):
                        ins = dve.tensor_scalar(pc_[:, c, 4 * i:4 * i + 4, :],
                                                TM[:, c, 64 * i:64 * i + 64].rearrange("p (m n) -> p m n", n=16
                                                                                       )[:, :, 0:NCMP],
                                                0.125, None, ALU.mult)
                chained(ins)
                masked = lambda at, i: bc(cst[:, at + i * NCMP:at + (i + 1) * NCMP].unsqueeze(1), [P, 4, NCMP])
                for c in range(2):
                    for i in range(NT):
                        ins = dve.tensor_tensor(pc_[:, c, 4 * i:4 * i + 4, :], pc_[:, c, 4 * i:4 * i + 4, :],
                                                masked(C_CMPN, i), ALU.add)
                chained(ins)
                spread = lambda k: bc(st8[:, k, 0:16].unsqueeze(2), [P, 16, NCMP])
                chained(dve.tensor_reduce(st8[:, 0, 0:16], pcf, AX, ALU.max))
                dve.tensor_tensor(pcf, pcf, spread(0), ALU.subtract).then_inc(s_cx, 1)
                mask_and_max(0, 0, PBf)
                dve.wait_ge(s_ce, t.next(s_ce))
                chained(dve.tensor_reduce(st8[:, 1, 0:16], pcf, AX, ALU.add))
                chained(dve.reciprocal(st8[:, 2, 0:16], st8[:, 1, 0:16]))
                for c in range(2):
                    view = lambda k: st8[:, k, 8 * c:8 * c + 8].rearrange("p (t h) -> p t h", t=NT)
                    ins = dve.tensor_tensor(view(3), view(2), gates[:, :, :, c, 0], ALU.mult)
                chained(ins)
                chained(dve.tensor_tensor(pcf, pcf, spread(3), ALU.mult))
                for c in range(2):
                    for i in range(NT):
                        ins = dve.tensor_tensor(pc_[:, c, 4 * i:4 * i + 4, :], pc_[:, c, 4 * i:4 * i + 4, :],
                                                masked(C_CMPM, i), ALU.mult)
                ins.then_inc(s_pc, 1)
                cut()
                for u in range(8):
                    gated(u, u // 4)
                    if u < 7:
                        mask_and_max(u + 1, (u + 1) // 4, PBf)
                    if u > 1:
                        cut()
                t.next(s_at, 2)
                low_out(xL[:, 4:8, :].rearrange("p d s -> p (d s)"), yT, xH[:, 4:8, :].rearrange("p d s -> p (d s)"))
                low_out(xL[:, 0:4, :].rearrange("p d s -> p (d s)"), PBf, xH[:, 0:4, :].rearrange("p d s -> p (d s)"))
                cut()
                for h in range(2):
                    cols_h = slice(h * 512, (h + 1) * 512)
                    dve.wait_ge(s_eaten, t.next("done", 14 if h == 0 else 2))
                    dve.tensor_tensor(xn[:, :, cols_h], (TM if h else GU)[:, :, :], sg_[0][:, :, cols_h], ALU.mult)
                    for i in range(NT):
                        ins = dve.tensor_tensor(y_[:, i, :], PY[:, 2 * i + h, :], sg_[1][:, i, cols_h], ALU.mult)
                    chained(ins)
                    dve.tensor_tensor(xn[:, :, cols_h], xn[:, :, cols_h], y_, ALU.add).then_inc(s_merged, 1)
                    cut()
                    d = slice(4 * h, 4 * h + 4)
                    low_out(xL[:, d, :].rearrange("p d s -> p (d s)"), TMf if h else GUf,
                            xH[:, d, :].rearrange("p d s -> p (d s)"))
                    cut()
                t.next(s_readA, 7)

            def out_norm(tile):
                by_head = lambda a: a.rearrange("p (g n) -> p g n", n=P)
                head_norm(by_head(GUf), 8, P, by_head(on_[tile]), by_head(xn[:, 0, :]))
                dve.sem_inc(s_readD, 1)
                dve.tensor_tensor(by_head(on_[tile]), by_head(on_[tile]), bc(vb[:, 2 * P:3 * P].unsqueeze(1),
                                  [P, 8, P]), ALU.mult).then_inc(s_on, 1)

            dve.memset(ones[:, :], 1.0).then_inc(s_ones, 1)
            dve.sem_inc(s_split, RING)
            dve.sem_inc(s_adafree, ADA_RING)
            dve.wait_ge(s_cs, 1)
            chained(dve.tensor_copy(cols[:, :], TM[:, 0, 0:P]))
            chained(dve.tensor_copy(peT[:, :], TM[:, 0, P:P + 64]))
            dve.wait_ge(s_col, 2)
            chained(dve.tensor_copy(bT[:, :], TM[:, 1, 0:4 * MODS]))
            for c in range(ADA_FIRST):
                start_products(0, 1)
                start_products(1, 2)
                ada_store(0, c, GU[:, c % 2, :])
            pieces = 0
            for n, (l, j) in enumerate(PHASES):
                if n == 0 or PHASES[n - 1][1] == 1:
                    cut()
                boundary(l, j, pieces)
                if j != 1:
                    ffn(l, j)
                elif l == 0:
                    hgrn()
                elif l == 1:
                    diff()
                else:
                    nsa(l)
                pieces = 3 * NF if j != 1 else PIECES[l] - (22 if l > 1 else 0)
            dve.wait_ge(s_gb, t.next(s_gb))
            dve.wait_ge(s_y, t.next(s_y))
            gated_output(0)
            add_output(0)
            dve.wait_ge(s_eaten, t.next("done", pieces))
            gated_output(1)
            add_output(1)
            if len(PHASES) == 12:
                dve.wait_ge(s_late, 16 * (N_LATE + 1))
                fg = ln_.rearrange("p a n -> p (a n)")
                for i in range(NT):
                    root(i)
                    dve.scalar_tensor_tensor(x[:, i, :], x[:, i, :], rstd[:, i:i + 1], fg, ALU.mult, ALU.mult
                                             ).then_inc(s_x, 1)

        @block.tensor
        def _(pe):
            t = Tally(s_split=RING)

            def times_three(outs, aH, aL, wh, wl, first, last):
                n = len(outs)
                for i in range(n):
                    pe.matmul(outs[i], aH, wh[i], start=first, stop=False)
                for i in range(n):
                    pe.matmul(outs[i], aH, wl[i], start=False, stop=False)
                for i in range(n):
                    ins = pe.matmul(outs[i], aL, wh[i], start=False, stop=last)
                return ins

            def gate_broadcast():
                pe.wait_ge(s_gcol, t.next(s_gcol))
                for d in range(ND):
                    ins = pe.matmul(TM[:, d // 4, (d % 4) * P:(d % 4 + 1) * P], shf[:, d * P:(d + 1) * P], ident,
                                    start=True, stop=True)
                ins.then_inc(s_gp, 1)

            def turn_x(i):
                pe.wait_ge(s_xn, t.next(s_xn))
                for d in range(ND):
                    ins = pe.matmul(PT[:, i, d, :], x[:, i, d * P:(d + 1) * P], diag[:, i, :], start=True, stop=True)
                    if d % 4 == 3:
                        ins.then_inc(s_xt, 1)

            def norm_and_first():
                gate_broadcast()
                turn_x(0)
                slots = [t.next("piece") % RING for _ in range(2)]
                pe.wait_ge(s_split, t.next(s_split, 2))
                for i in range(NT):
                    toks = slice(i * P, (i + 1) * P)
                    for d in range(ND):
                        if d % 2 == 0:
                            pe.wait_ge(s_xl, t.next(s_xl))
                        slot, b = slots[d // 4], slice(d % 4 * 512, (d % 4 + 1) * 512)
                        ins = times_three([GU[:, i, :]], xH[:, d, toks], xL[:, d, toks], [wH[:, slot, b]],
                                          [wL[:, slot, b]], d == 0, d == ND - 1)
                        if i == 1 and d % 4 == 3:
                            ins.then_inc(s_eaten, 1)
                        if i == 0 and d == 5:
                            turn_x(1)
                pe.wait_ge(s_gb, t.next(s_gb))

            def up(q):
                by_token([GU[:, i, :] for i in range(NT)], q)

            def turn_hidden():
                for i in range(NT):
                    for f in range(2):
                        ins = pe.transpose(TM[:, 0, f * S + i * P:f * S + (i + 1) * P],
                                           sh[:, 1, i, f * P:(f + 1) * P], ident)
                ins.then_inc(s_ht, 1)

            def down(first, last):
                slot = t.next("piece") % RING
                pe.wait_ge(s_split, t.next(s_split))
                pe.wait_ge(s_hl, t.next(s_hl))
                for i in range(NT):
                    for f in range(2):
                        a = slice(i * P, (i + 1) * P)
                        halves = [slice(f * D + h * 512, f * D + (h + 1) * 512) for h in range(2)]
                        ins = times_three([PY[:, 2 * i + h, :] for h in range(2)], hH[:, f, a], hL[:, f, a],
                                          [wH[:, slot, b] for b in halves], [wL[:, slot, b] for b in halves],
                                          first and f == 0, last and f == 1)
                    if last and i == 0:
                        ins.then_inc(s_y, 1)
                ins.then_inc(s_eaten, 1)

            def ada_sums(bank=TM[:, 1, :], fresh=True):
                pe.wait_ge(s_acc, t.next(s_acc))
                for k in range(4):
                    ins = pe.matmul(bank[:, k:k + 1], acc[:, k * P:(k + 1) * P], ones[:, :], start=fresh, stop=True,
                                    skip_group_check=not fresh)
                ins.then_inc(s_modp, 1)

            def ada_direct(c, q, tiles):
                slot = t.next("start") % START_RING
                pe.wait_ge(s_start[slot], t.next(s_start[slot], 16))
                for k in tiles:
                    for n in range(4):
                        w = start_[slot][:, k * 512 + n * P:k * 512 + (n + 1) * P]
                        ins = pe.matmul(GU[:, c % 2, n:n + 1], w, cs[:, 4 * q + k:4 * q + k + 1],
                                        start=(q == 0 and k == tiles[0] and n == 0), stop=False,
                                        skip_group_check=True)
                ins.then_inc(s_direct, 1)

            def ffn(l, j):
                norm_and_first()

                def turn(with_ada, first=False):
                    pe.wait_ge(s_h, t.next(s_h))
                    up(0)
                    turn_hidden()
                    up(1)
                    if with_ada:
                        ada_sums()
                    down(first, False)

                def loop(count, with_ada):
                    with pe.Fori(0, count) as i:
                        t.enter(i, [("piece", 3), (s_split, 3), (s_h, 1), (s_hl, 1), (s_acc, int(with_ada))])
                        turn(with_ada)
                    t.leave(count)

                turns = ada_turns(l, j)[2]
                turn(turns > 0, True)
                if turns:
                    loop(turns - 1, True)
                rest = NF - 1 - max(turns, 1)
                if rest:
                    loop(rest, False)
                pe.wait_ge(s_h, t.next(s_h))
                turn_hidden()
                down(False, True)

            def by_token(banks, q, width=512, tiles=(0, ND - 1), end=False):
                slot = t.next("piece") % RING
                pe.wait_ge(s_split, t.next(s_split))
                for i in range(NT):
                    for k in range(4):
                        d = 4 * q + k
                        a, b = slice(i * P, (i + 1) * P), slice(k * width, (k + 1) * width)
                        ins = times_three([banks[i]], xH[:, d, a], xL[:, d, a], [wH[:, slot, b]], [wL[:, slot, b]],
                                          d == tiles[0], d == tiles[1])
                    if end and i == 0:
                        ins.then_inc(s_y, 1)
                ins.then_inc(s_eaten, 1)

            def by_channel(banks, q):
                slot = t.next("piece") % RING
                pe.wait_ge(s_split, t.next(s_split))
                for k in range(4):
                    d = 4 * q + k
                    for n in range(4):
                        w = slice(k * 512 + n * P, k * 512 + (n + 1) * P)
                        o = banks[:, n * S:(n + 1) * S]
                        pe.matmul(o, wH[:, slot, w], xH[:, d, :], start=(d == 0 and n % 2 == 0), stop=False,
                                  skip_group_check=True)
                        pe.matmul(o, wH[:, slot, w], xL[:, d, :], start=False, stop=False, skip_group_check=True)
                        ins = pe.matmul(o, wL[:, slot, w], xH[:, d, :], start=False, stop=(d == ND - 1),
                                        skip_group_check=True)
                ins.then_inc(s_eaten, 1)

            def project(q, h):
                by_token([PY[:, 2 * i + h, :] for i in range(NT)], q, end=(q == 1 and h == 1))

            def hgrn():
                norm_and_first()
                A, B = [GU[:, i, :] for i in range(NT)], [PY[:, i, :] for i in range(NT)]
                by_channel(PAf, 0)
                by_channel(PAf, 1)
                pe.wait_ge(s_readA, t.next(s_readA))
                by_channel(GUf, 0)
                by_channel(GUf, 1)
                pe.wait_ge(s_readD, t.next(s_readD))
                by_token(B, 0)
                by_token(B, 1)
                for grp in range(2):
                    if grp == 1:
                        pe.wait_ge(s_readD, t.next(s_readD, 2))
                    for n in range(9):
                        if n:
                            pe.wait_ge(s_z, t.next(s_z))
                        if n > 1:
                            pe.wait_ge(s_sel, t.next(s_sel))
                        dst = (PBf if n % 2 == 0 else TMf).rearrange("p (h s) -> p h s", s=P)
                        e = E[n % 3].rearrange("p (h s) -> p h s", s=P)
                        kk, qq = (k_.rearrange("p (h s) -> p h s", s=P), q_.rearrange("p (h s) -> p h s", s=P)
                                  ) if n == 0 else (e, e)
                        for h in range(8 if n < 8 else 4):
                            if n < 8:
                                ins = pe.matmul(dst[:, h, :], kk[:, h, :], qq[:, h, :], start=True, stop=True)
                            else:
                                ins = pe.matmul(dst[:, h, :], kk[:, 2 * h, :], qq[:, 2 * h + 1, :],
                                                start=True, stop=True)
                        ins.then_inc(s_gram, 1)
                        if grp == 0 and n < 8:
                            if n == 0:
                                pe.wait_ge(s_readD, t.next(s_readD))
                            if n == 2:
                                pe.wait_ge(s_readA, t.next(s_readA))
                            if n == 4 or n == 6:
                                pe.wait_ge(s_readA, t.next(s_readA))
                            if n < 4:
                                by_token(A if n < 2 else B, n % 2)
                            else:
                                by_channel(GUf if n < 6 else PAf, n % 2)
                    pe.wait_ge(s_sel, t.next(s_sel, 2))
                    for h in range(4):
                        c = slice((4 * grp + h) * P, (4 * grp + h + 1) * P)
                        pe.matmul(TM[:, 0, h * P:(h + 1) * P], att[:, 2 * h, :], v_[:, 0, c], start=True, stop=True)
                        pe.matmul(TM[:, 1, h * P:(h + 1) * P], att[:, 2 * h + 1, :], v_[:, 1, c],
                                  start=True, stop=False)
                        ins = pe.matmul(TM[:, 1, h * P:(h + 1) * P], attX[:, h, :], v_[:, 0, c],
                                        start=False, stop=True)
                    ins.then_inc(s_o, 1)
                    if grp == 1:
                        pe.wait_ge(s_xl, t.next(s_xl))
                        project(0, 0)
                        project(0, 1)
                    pe.wait_ge(s_on, t.next(s_on))
                    for h in range(4):
                        for i in range(NT):
                            ins = pe.transpose((GUf if grp else PBf)[:, h * S + i * P:h * S + (i + 1) * P],
                                               q_[:, i * 512 + h * P:i * 512 + (h + 1) * P], ident)
                    ins.then_inc(s_ot, 1)
                pe.wait_ge(s_xl, t.next(s_xl))
                project(1, 0)
                project(1, 1)

            def scores(u, tile, keys, heads, queries=qT, double=True):
                banks = (PAf if double and u % 2 else PBf).rearrange("p (m s) -> p m s", s=S)
                if u > double:
                    pe.wait_ge(s_scored, t.next(s_scored))
                for n, h in enumerate(heads):
                    for c in range(2):
                        r = slice(c * 64, (c + 1) * 64)
                        ins = pe.matmul(banks[:, 2 * c + n, 0:P * (tile + 1)], queries[r, h, tile * P:(tile + 1) * P],
                                        keys(h)[r, 0:P * (tile + 1)], start=True, stop=True)
                ins.then_inc(s_score, 1)

            def turn_weights(u, tile, maps):
                pe.wait_ge(s_a, t.next(s_a))
                for h in range(2):
                    for k in range(tile + 1):
                        n = h * (tile + 1) + k
                        ins = pe.transpose(TM[:, u % 2, n * P:(n + 1) * P], a_[u % 2][:, h, k * P:(k + 1) * P], ident)
                ins.then_inc(s_at, 1)

            def diff():
                norm_and_first()
                A, B = [GU[:, i, :] for i in range(NT)], [PY[:, i, :] for i in range(NT)]
                keys = lambda h: kT[:, h, :]
                heads = lambda u: (2 * (u % 4), 2 * (u % 4) + 1)
                for c in range(1, 6):
                    if c > 1:
                        pe.wait_ge(s_readD, t.next(s_readD))
                    for q in range(2):
                        if c == 5 and q == 1:
                            pe.wait_ge(s_aT, t.next(s_aT))
                            scores(0, 0, keys, heads(0))
                        by_token(B if c % 2 else A, q)
                    turn_chunk(c - 1)
                pe.wait_ge(s_readA, t.next(s_readA, 2))
                scores(1, 0, keys, heads(1))
                for u in range(8):
                    tile = u // 4
                    turn_weights(u, tile, 2)
                    if u < 6:
                        scores(u + 2, (u + 2) // 4, keys, heads(u + 2))
                    if u == 4:
                        pe.wait_ge(s_readD, t.next(s_readD))
                    pe.wait_ge(s_aT, t.next(s_aT))
                    for n, h in enumerate(heads(u)):
                        for k in range(tile + 1):
                            m = n * (tile + 1) + k
                            ins = pe.matmul(GUf[:, h * P:(h + 1) * P], aT[u % 2][:, m * P:(m + 1) * P],
                                            vB[:, k, h * P:(h + 1) * P], start=(k == 0), stop=(k == tile))
                    if u % 4 == 3:
                        ins.then_inc(s_o, 1)
                t.next(s_scored, 2)
                pe.wait_ge(s_readD, t.next(s_readD))
                pe.wait_ge(s_on, t.next(s_on, 2))
                for d in range(ND):
                    for i in range(NT):
                        ins = pe.transpose(PYt[:, d, i * P:(i + 1) * P], on_[i][:, d * P:(d + 1) * P], ident)
                    if d % 2:
                        ins.then_inc(s_ot, 1)
                pe.wait_ge(s_xl, t.next(s_xl, 4))
                for h in range(2):
                    for q in range(2):
                        project(q, h)

            def turn_chunk(c):
                if c > 3:
                    return
                pe.wait_ge(s_on, t.next(s_on))
                if c:
                    pe.wait_ge(s_aT, t.next(s_aT))
                for h in range(4):
                    for i in range(NT):
                        ins = pe.transpose(TMf[:, h * S + i * P:h * S + (i + 1) * P],
                                           qk_[:, i * 512 + h * P:i * 512 + (h + 1) * P], ident)
                ins.then_inc(s_ot, 1)

            def turn_tiles(dst, src):
                for d in range(4):
                    for i in range(NT):
                        ins = pe.transpose(dst[:, d * S + i * P:d * S + (i + 1) * P], src(i, d), ident)
                ins.then_inc(s_ot, 1)

            def nsa(l):
                norm_and_first()
                A, B = [GU[:, i, :] for i in range(NT)], [PY[:, i, :] for i in range(NT)]

                def chunk(banks, width=512):
                    for q in range(2):
                        by_token([b[:, 0:width] for b in banks], q, width)

                chunk(B)
                pe.wait_ge(s_on, t.next(s_on))
                turn_tiles(TMf, lambda i, m: cd_[:, i, m].rearrange("p c n -> p (c n)"))
                pe.wait_ge(s_readD, t.next(s_readD))
                chunk(A, width=280)
                pe.wait_ge(s_on, t.next(s_on))
                pe.wait_ge(s_aT, t.next(s_aT))
                turn_tiles(TMf, lambda i, h: qr_[:, i, h * P:(h + 1) * P])
                pe.wait_ge(s_w1, 80 * (l - 1))
                for j in range(2):
                    for n in range(16):
                        w = w1_[j][:, n * P:(n + 1) * P]
                        pe.matmul(PY[:, 2, 64 * j:64 * j + 30], w, cT_[:, j, :, 2 * n:2 * n + 16 * (NCMP - 1) + 1:16],
                                  start=(n == 0), stop=(n == 15))
                    for n in range(16):
                        w = w1_[j][:, n * P:(n + 1) * P]
                        at = (l - 2) * 32 + j * 16 + n
                        ins = pe.matmul(PY[:, 2, 64 * j + 32:64 * j + 33], w, peT[:, at:at + 1],
                                        start=(n == 0), stop=(n == 15))
                ins.then_inc(s_cmp, 1)
                pe.wait_ge(s_readD, t.next(s_readD))
                chunk(B)
                pe.wait_ge(s_hc, t.next(s_hc))
                for j in range(2):
                    for g in range(2):
                        m = 2 * j + g
                        ins = pe.matmul(PY[0:NCMP, 3, m * 64:(m + 1) * 64], hc_[:, j, g * NCMP:(g + 1) * NCMP],
                                        w2_[:, j, :], start=True, stop=True)
                ins.then_inc(s_cmp, 1)
                pe.wait_ge(s_on, t.next(s_on))
                pe.wait_ge(s_aT, t.next(s_aT))
                turn_tiles(TMf, lambda i, m: kd_[:, m // 2, i, m % 2].rearrange("p c n -> p (c n)"))
                pe.wait_ge(s_readD, t.next(s_readD))
                chunk(A)
                pe.wait_ge(s_kc, t.next(s_kc))
                for g in range(2):
                    ins = pe.transpose(PY[:, 2, g * 16:g * 16 + NCMP],
                                       kcd[0:NCMP, g].rearrange("p c n -> p (c n)"), ident[0:NCMP, 0:NCMP])
                ins.then_inc(s_cmp, 1)
                pe.wait_ge(s_wm, t.next(s_wm))
                pe.wait_ge(s_aT, t.next(s_aT))
                for g in range(8):
                    ins = pe.transpose(TMf[:, g * P:(g + 1) * P], ws_[:, g, :], ident)
                ins.then_inc(s_ot, 1)
                pe.wait_ge(s_vn, t.next(s_vn))
                pe.wait_ge(s_kc, t.next(s_kc))
                pe.wait_ge(s_aT, t.next(s_aT))
                for g in range(8):
                    for i in range(NT):
                        ins = pe.matmul(PY[:, 2 + i, g * 64:(g + 1) * 64], wsT[:, g * P:(g + 1) * P],
                                        vg_[:, i, g * 64:(g + 1) * 64], start=True, stop=True)
                ins.then_inc(s_sv, 1)
                pe.wait_ge(s_readA, t.next(s_readA))
                by_token(B, 0)
                pe.wait_ge(s_yb, t.next(s_yb))
                turn_tiles(PBf, lambda i, d: y_[:, i, d * P:(d + 1) * P])
                for i in range(NT):
                    for h in range(4):
                        for c in range(2):
                            r = slice(c * 64, (c + 1) * 64)
                            at = 64 * i + 16 * h
                            ins = pe.matmul(TM[:, c, at:at + NCMP], qT2[r, h, i * P:(i + 1) * P],
                                            kcT[r, h // 2, 0:NCMP], start=True, stop=True)
                ins.then_inc(s_cmp, 1)
                keys = lambda u: (lambda h: kT2[:, u % 2, u // 2 % 2, :])
                pairs = lambda u: (u // 2 % 2 * 2, u // 2 % 2 * 2 + 1)
                pe.wait_ge(s_aT, t.next(s_aT))
                scores(0, 0, keys(0), pairs(0), qT2, False)
                by_token(B, 1)
                pe.wait_ge(s_pc, t.next(s_pc))
                for i in range(NT):
                    if i:
                        pe.wait_ge(s_aT, t.next(s_aT))
                    for h in range(8):
                        ins = pe.transpose(TMf[0:NCMP, h * P:(h + 1) * P], pc_[:, h % 2, 4 * i + h // 2, :], ident)
                    ins.then_inc(s_ot, 1)
                pe.wait_ge(s_readA, t.next(s_readA))
                pe.wait_ge(s_aT, t.next(s_aT))
                for i in range(NT):
                    for h in range(8):
                        pe.matmul(GU[:, i, h * 64:(h + 1) * 64], xn[0:NCMP, i, h * P:(h + 1) * P],
                                  vc_[0:NCMP, h // 4, :], start=(h == 0), stop=False, skip_group_check=True)
                for u in range(8):
                    tile, g, b = u // 4, u // 2 % 2, u % 2
                    pe.wait_ge(s_a, t.next(s_a))
                    for m in range(4):
                        for k in range(tile + 1):
                            dst = TMf[:, (2 * m + k) * P:(2 * m + k + 1) * P] if tile else \
                                TM[:, u % 2, m * P:(m + 1) * P]
                            ins = pe.transpose(dst, a2_[u % 2][:, m, k * P:(k + 1) * P], ident)
                    ins.then_inc(s_at, 1)
                    if u < 7:
                        scores(u + 1, (u + 1) // 4, keys(u + 1), pairs(u + 1), qT2, False)
                    if 1 <= u <= 6:
                        if u % 2:
                            pe.wait_ge(s_readA, t.next(s_readA))
                        by_token(B, (u + 1) % 2)
                    pe.wait_ge(s_aT, t.next(s_aT))
                    for m in range(4):
                        h = 2 * (2 * g + m % 2) + m // 2
                        for k in range(tile + 1):
                            n = m * (tile + 1) + k
                            ins = pe.matmul(GU[:, tile, h * 64:(h + 1) * 64], aT2[u % 2][:, n * P:(n + 1) * P],
                                            v2_[:, b, k, g * 64:(g + 1) * 64], start=False,
                                            stop=(b == 1 and k == tile), skip_group_check=True)
                    if u % 4 == 3:
                        ins.then_inc(s_o, 1)
                pe.wait_ge(s_scored, t.next(s_scored))
                pe.wait_ge(s_readA, t.next(s_readA, 3))
                turn_tiles(PBf, lambda i, d: yo_[:, i, d * P:(d + 1) * P])
                pe.wait_ge(s_xl, t.next(s_xl, 2))
                halves = [[PY[:, 2 * i + h, :] for i in range(NT)] for h in range(2)]
                by_token(A, 0, tiles=(0, 3))
                by_token(halves[0], 1, tiles=(4, 7))
                by_token([TM[:, i, :] for i in range(NT)], 0, tiles=(0, 3))
                pe.wait_ge(s_merged, t.next(s_merged))
                turn_tiles(GUf, lambda i, d: xn[:, i, d * P:(d + 1) * P])
                by_token(halves[1], 1, tiles=(4, 7))
                pe.wait_ge(s_xl, t.next(s_xl))
                project(0, 0)
                pe.wait_ge(s_merged, t.next(s_merged))
                turn_tiles(TMf, lambda i, d: xn[:, i, (4 + d) * P:(5 + d) * P])
                project(0, 1)
                pe.wait_ge(s_xl, t.next(s_xl))
                project(1, 0)
                project(1, 1)

            pe.sem_inc(s_eaten, RING)
            pe.wait_ge(s_ones, 1)
            pe.wait_ge(s_const, N_CONST * 16)
            pe.transpose(TM[:, 0, 0:P], rows[:, 0, :], ident)
            pe.transpose(TM[:, 0, P:P + 64], rows[0:64, 5, :], ident[0:64, 0:64]).then_inc(s_col, 1)
            for l in range(4):
                ins = pe.transpose(TM[:, 1, l * MODS:(l + 1) * MODS], rows[0:MODS, 1 + l, :], ident[0:MODS, 0:MODS])
            ins.then_inc(s_col, 1)
            pe.wait_ge(s_cs, 1)
            for c in range(ADA_FIRST):
                ada_direct(c, 0, (3,))
                ada_direct(c, 1, (2, 3))
                ada_sums(GU[:, c % 2, :], False)
            for l, j in PHASES:
                if j != 1:
                    ffn(l, j)
                elif l == 0:
                    hgrn()
                elif l == 1:
                    diff()
                else:
                    nsa(l)


def table():
    import numpy as np
    a = np.zeros((P, C_END), np.float32)
    p = np.arange(P)
    a[:, C_ID:C_ID + P] = np.eye(P)
    a[:, C_CAUSAL:C_CAUSAL + P] = np.where(p[None, :] <= p[:, None], 0.0, NEG)
    a[:, C_TRIL:C_TRIL + P] = p[None, :] <= p[:, None]
    a[:, C_SCAN:C_SCAN + 4 * S] = np.arange(4 * S) % 64 != 0
    for n in range(NLEVEL):
        m = 1 << n
        a[:, C_LEVEL + n * P:C_LEVEL + (n + 1) * P] = ((p[:, None] // (2 * m) == p[None, :] // (2 * m))
                                                       & (p[:, None] // m % 2 == 0) & (p[None, :] // m % 2 == 1))
    ends = np.arange(NCMP) * 16 + 31
    token = np.arange(S)
    seen = (ends[None, :] <= token[:, None]).reshape(NT, P, NCMP).transpose(1, 0, 2).reshape(P, -1)
    a[:, C_CMPM:C_CMPM + NT * NCMP] = seen
    a[:, C_CMPN:C_CMPN + NT * NCMP] = np.where(seen, 0.0, NEG)
    inv = np.float32(1.0) / (10000.0 ** (np.arange(0, 64, 2) / 64)).astype(np.float32)
    for at, f in ((C_COS, np.cos), (C_SIN, np.sin)):
        v = f((token.astype(np.float32)[:, None] * inv[None, :]).astype(np.float64))
        a[:, at:at + NT * 32] = v.reshape(NT, P, 32).transpose(1, 0, 2).reshape(P, -1)
    for at, f in ((C_CCOS, np.cos), (C_CSIN, np.sin)):
        a[0:NCMP, at:at + 32] = f((ends.astype(np.float32)[:, None] * inv[None, :]).astype(np.float64))
    a[:, C_FREQ:C_FREQ + 8] = 500000.0 ** (-np.arange(0, 16, 2) / 16)
    return a


_INS = ["x", "positions", "ada_w", "ada_b", "ffn_wi", "ffn_wo", "a_w_in", "a_w_out", "a_onorm", "b_w_in", "b_w_out",
        "b_qk_g", "b_lam", "b_subln", "ada_w_2", "ada_b_2", "ffn_w_in_2", "ffn_w_out_2", "mix_w_in_2",
        "cmp_pe_2", "cmp_w1_2", "cmp_w2_2", "gm_ln_g_2", "gm_ln_b_2", "gm_ws_2", "proj_a_2", "proj_b_2", "w_out_2",
        "final_g_2"]


def kernel(**inputs):
    import numpy as _np
    import concourse.bacc as _bacc
    from concourse.bass_utils import run_bass_kernel_spmd as _run

    nc = _bacc.Bacc("TRN2", target_bir_lowering=False, num_devices=1)
    arrays, tensors = {}, {}
    given = {name: _np.ascontiguousarray(inputs[name]) for name in _INS}
    given["vec_rows"] = _np.concatenate([_np.asarray(inputs[n]).reshape(-1, P) for n in
                                         ("c", "c_2", "norm_g", "norm_g_2", "gm_bs_2")])
    given["table"] = table()
    for name, a in given.items():
        arrays[f"in_{name}"] = a
        tensors[name] = nc.dram_tensor(f"in_{name}", a.shape, mybir.dt.from_np(a.dtype), kind="ExternalInput").ap()
    out = nc.dram_tensor("out", (1, S, D), F32, kind="ExternalOutput").ap()
    build(nc, tensors, out)
    r = _run(nc, [arrays], core_ids=[0])
    return r.results[0]["out"]
```
